# Optimizing a Trainium2 kernel written in Bass

```python
import math
import jax, jax.numpy as jnp
from jax import lax
import numpy as np

D_MODEL = 1024
BATCH = 1
SEQ = 1024
DEPTH = 2
DEC_BATCH = 8
DEC_SEQ = 4
PAST_LEN = 2048
PAGE_SIZE = 128

N_EVEN = (DEPTH + 1) // 2
N_ODD = DEPTH // 2
EPS = 1e-6

A_HEAD_DIM = 64
A_HEADS_PER_GROUP = 4
A_GROUPS = ((128, 1), (512, 4), (2048, 16))
A_N_GROUPS = len(A_GROUPS)
A_HEADS = A_N_GROUPS * A_HEADS_PER_GROUP
A_OUT = A_HEADS_PER_GROUP * A_HEAD_DIM
A_QKV = 3 * A_HEADS * A_HEAD_DIM
A_BLOCK = 128
A_SCALE = A_HEAD_DIM ** -0.5
N_BUCKETS = 32
BUCKET_MAX_DIST = 2048

B_HEAD_DIM = 64
B_HEADS = 12
B_WIDTH = B_HEADS * B_HEAD_DIM
DECAY_LORA = 64
AAA_LORA = 64
GATE_LORA = 160
B_COLS = 3 * B_WIDTH + DECAY_LORA + AAA_LORA + GATE_LORA
E_COLS = A_QKV + B_COLS
MIX_WIDTH = A_OUT + B_WIDTH
LNX_EPS = 64e-5

C_EXPAND = 128
C_HEADS = D_MODEL // C_EXPAND
C_FDIM = C_HEADS * C_EXPAND
C_VDIM_HEAD = D_MODEL // C_HEADS
C_COLS = 2 * C_FDIM + 2 * D_MODEL
C_CHUNK = 64

D_FF = 4 * D_MODEL

kernel_name = 'hybrid_dilated_rwkv7_hgrn2_step'

def rmsnorm(x, g):
    xf = x.astype(jnp.float32)
    y = xf * lax.rsqrt(jnp.mean(xf * xf, -1, keepdims=True) + EPS)
    return (y * g.astype(jnp.float32)).astype(x.dtype)

def t5_bucket(dist):
    max_exact = N_BUCKETS // 2
    d = jnp.maximum(dist, 1).astype(jnp.float32)
    large = max_exact + (jnp.log(d / max_exact) / math.log(BUCKET_MAX_DIST / max_exact)
                         * (N_BUCKETS - max_exact)).astype(jnp.int32)
    large = jnp.minimum(large, N_BUCKETS - 1)
    return jnp.where(dist < max_exact, dist, large)

def dilated_block(q, kv, pos0, bias, window, dil):
    T = q.shape[1]
    nk = window // dil + 1
    t = jnp.arange(T)
    j = jnp.arange(nk)
    rows = window + t[:, None] - j[None, :] * dil
    valid = (pos0 + t[:, None] - j[None, :] * dil) >= 0
    kvg = kv[:, rows].astype(jnp.float32)
    logits = jnp.einsum('bthd,btjhd->bhtj', q.astype(jnp.float32), kvg[:, :, :, 0]) * A_SCALE
    logits = logits + bias.T[None, :, None, :]
    logits = jnp.where(valid[None, None], logits, -jnp.inf)
    lse = jax.nn.logsumexp(logits, axis=-1)
    p = jnp.exp(logits - lse[..., None])
    o = jnp.einsum('bhtj,btjhd->bthd', p, kvg[:, :, :, 1])
    return o, lse

def attend_group(q, kv_full, pos0, bias, window, dil):
    B_, T, H, Dh = q.shape
    if T <= A_BLOCK:
        return dilated_block(q, kv_full, pos0, bias, window, dil)
    nb = T // A_BLOCK

    def one(n):
        s = n * A_BLOCK
        qb = lax.dynamic_slice_in_dim(q, s, A_BLOCK, axis=1)
        kvb = lax.dynamic_slice_in_dim(kv_full, s, window + A_BLOCK, axis=1)
        return dilated_block(qb, kvb, pos0 + s, bias, window, dil)

    o, lse = lax.map(one, jnp.arange(nb))
    o = jnp.moveaxis(o, 0, 1).reshape(B_, T, H, Dh)
    lse = jnp.moveaxis(lse, 0, 2).reshape(B_, H, T)
    return o, lse

def mixer_a(qkv, pos0, rel_bias, fronts):
    B_, T = qkv.shape[:2]
    outs, lses, rows = [], [], []
    for g, (window, dil) in enumerate(A_GROUPS):
        hs = slice(g * A_HEADS_PER_GROUP, (g + 1) * A_HEADS_PER_GROUP)
        q = qkv[:, :, 0, hs]
        kv_new = qkv[:, :, 1:, hs]
        kv_full = jnp.concatenate([fronts[g].astype(kv_new.dtype), kv_new], axis=1)
        nk = window // dil + 1
        bias = rel_bias[t5_bucket(jnp.arange(nk) * dil)][:, hs].astype(jnp.float32)
        o, lse = attend_group(q, kv_full, pos0, bias, window, dil)
        outs.append(o)
        lses.append(lse)
        rows.append(kv_new[:, -min(window, T):])
    wts = jax.nn.softmax(jnp.stack(lses), axis=0)
    out = jnp.einsum('gbht,gbthd->bthd', wts, jnp.stack(outs))
    return out.reshape(B_, T, A_OUT), rows

def mixer_b(pb, shift_prev, s0, mu, w0, w2, a0, a2, g2, k_k, k_a, r_k, lnx_w, lnx_b):
    f32 = jnp.float32
    B_, T, _ = pb.shape
    pb = pb.astype(f32)
    prev = jnp.concatenate([shift_prev.astype(f32)[:, None], pb[:, :-1]], axis=1)
    xs = pb + (prev - pb) * mu.astype(f32)
    W = B_WIDTH
    r = xs[..., :W]
    k = xs[..., W:2 * W]
    v = xs[..., 2 * W:3 * W]
    wd = xs[..., 3 * W:3 * W + DECAY_LORA]
    ad = xs[..., 3 * W + DECAY_LORA:3 * W + DECAY_LORA + AAA_LORA]
    gd = xs[..., 3 * W + DECAY_LORA + AAA_LORA:]
    w = -jax.nn.softplus(-(w0.astype(f32) + jnp.tanh(wd) @ w2.astype(f32))) - 0.5
    decay = jnp.exp(-jnp.exp(w))
    a = jax.nn.sigmoid(a0.astype(f32) + ad @ a2.astype(f32))
    g = jax.nn.sigmoid(gd) @ g2.astype(f32)
    heads = lambda t: t.reshape(B_, T, B_HEADS, B_HEAD_DIM)
    kk = heads(k * k_k.astype(f32))
    kk = kk / jnp.maximum(jnp.sqrt(jnp.sum(kk * kk, -1, keepdims=True)), 1e-12)
    k = k * (1.0 + (a - 1.0) * k_a.astype(f32))
    r_h, k_h, v_h, d_h, a_h = heads(r), heads(k), heads(v), heads(decay), heads(a)
    tm = lambda t: jnp.moveaxis(t, 1, 0)

    def step(S, inp):
        r_t, d_t, k_t, v_t, kk_t, a_t = inp
        sa = jnp.einsum('bhvk,bhk->bhv', S, -kk_t)
        S = (S * d_t[:, :, None, :] + sa[..., None] * (kk_t * a_t)[:, :, None, :]
             + v_t[..., None] * k_t[:, :, None, :])
        return S, jnp.einsum('bhvk,bhk->bhv', S, r_t)

    S, y = lax.scan(step, s0.astype(f32), (tm(r_h), tm(d_h), tm(k_h), tm(v_h), tm(kk), tm(a_h)))
    y = tm(y)
    mean = jnp.mean(y, -1, keepdims=True)
    var = jnp.mean(jnp.square(y - mean), -1, keepdims=True)
    y = ((y - mean) * lax.rsqrt(var + LNX_EPS)).reshape(B_, T, W) * lnx_w.astype(f32) + lnx_b.astype(f32)
    bonus = jnp.sum(r_h * k_h * r_k.astype(f32), -1, keepdims=True) * v_h
    out = (y + bonus.reshape(B_, T, W)) * g
    return out, pb[:, -1], S

def hgrn_lower_bounds(lb_raw):
    sm = jax.nn.softmax(lb_raw.astype(jnp.float32), axis=0)
    return jnp.cumsum(sm, axis=0) - sm[0]

def gla_chunks(q, k, v, logf, s0, chunk):
    B_, T, H, Dk = q.shape
    Dv = v.shape[-1]
    n = T // chunk
    to_chunks = lambda t: jnp.moveaxis(t.reshape(B_, n, chunk, H, t.shape[-1]), 1, 0)
    mask = jnp.tril(jnp.ones((chunk, chunk), bool))[None, :, :, None, None]

    def step(S, inp):
        qc, kc, vc, lc = inp
        b = jnp.cumsum(lc, axis=1)
        diff = b[:, :, None] - b[:, None, :]
        dec = jnp.exp(jnp.where(mask, diff, -jnp.inf))
        att = jnp.einsum('bthk,bshk,btshk->bhts', qc, kc, dec)
        o = (jnp.einsum('bthk,bhkv->bthv', qc * jnp.exp(b), S)
             + jnp.einsum('bhts,bshv->bthv', att, vc))
        bl = b[:, -1]
        S = S * jnp.exp(bl)[..., None] + jnp.einsum('bshk,bshv->bhkv', kc * jnp.exp(bl[:, None] - b), vc)
        return S, o

    S, o = lax.scan(step, s0, (to_chunks(q), to_chunks(k), to_chunks(v), to_chunks(logf)))
    return jnp.moveaxis(o, 0, 1).reshape(B_, T, H, Dv), S

def mixer_c(pc, s0, lb, norm_g):
    f32 = jnp.float32
    B_, T, _ = pc.shape
    pc = pc.astype(f32)
    q = jax.nn.silu(pc[..., :C_FDIM])
    fg = lb + (1.0 - lb) * jax.nn.sigmoid(pc[..., C_FDIM:2 * C_FDIM])
    k = 1.0 - fg
    logf = jnp.log(fg)
    i = pc[..., 2 * C_FDIM:2 * C_FDIM + D_MODEL]
    gate = pc[..., 2 * C_FDIM + D_MODEL:]
    hk = lambda t: t.reshape(B_, T, C_HEADS, C_EXPAND)
    chunk = C_CHUNK if T % C_CHUNK == 0 else T
    o, S = gla_chunks(hk(q), hk(k), i.reshape(B_, T, C_HEADS, C_VDIM_HEAD), hk(logf), s0.astype(f32), chunk)
    o = rmsnorm(o.reshape(B_, T, D_MODEL), norm_g) * jax.nn.silu(gate)
    return o, S

def trunk(x, pos0, a_fronts, b_shift0, b_state0, c_state0, p):
    B_, T, _ = x.shape
    dt = x.dtype
    lb_all = hgrn_lower_bounds(p['c_lb_raw'])
    kv_rows = [[] for _ in A_GROUPS]
    shifts, wkvs, cstates = [], [], []
    for layer in range(DEPTH):
        h = rmsnorm(x, p['norm_mix'][layer])
        if layer % 2 == 0:
            e = layer // 2
            proj = h @ p['e_w_in'][e]
            qkv = proj[..., :A_QKV].reshape(B_, T, 3, A_HEADS, A_HEAD_DIM)
            a_out, rows = mixer_a(qkv, pos0, p['rel_bias'], [f[e] for f in a_fronts])
            b_out, shift, wkv = mixer_b(proj[..., A_QKV:], b_shift0[e], b_state0[e], p['e_mu'][e],
                                        p['e_w0'][e], p['e_w2'][e], p['e_a0'][e], p['e_a2'][e],
                                        p['e_g2'][e], p['e_k_k'][e], p['e_k_a'][e], p['e_r_k'][e],
                                        p['e_lnx_w'][e], p['e_lnx_b'][e])
            for g in range(A_N_GROUPS):
                kv_rows[g].append(rows[g])
            shifts.append(shift)
            wkvs.append(wkv)
            mix = jnp.concatenate([a_out, b_out], -1).astype(dt) @ p['e_w_out'][e]
        else:
            o = layer // 2
            c_out, sc = mixer_c(h @ p['c_w_in'][o], c_state0[o], lb_all[layer], p['c_norm'][o])
            cstates.append(sc)
            mix = c_out.astype(dt) @ p['c_w_out'][o]
        x = x + mix.astype(dt)
        h = rmsnorm(x, p['norm_mlp'][layer])
        x = x + (jnp.square(jax.nn.relu(h @ p['mlp_up'][layer])) @ p['mlp_down'][layer]).astype(dt)
    y = rmsnorm(x, p['norm_final'])
    return y, [jnp.stack(r) for r in kv_rows], jnp.stack(shifts), jnp.stack(wkvs), jnp.stack(cstates)

def setup_inputs(seed: int = 0) -> dict:
    key = jax.random.key(seed)
    ks = iter(jax.random.split(key, 40))
    nrm = lambda shape, s: jax.random.normal(next(ks), shape, jnp.float32) * s
    L = [min(w, PAST_LEN) for w, _ in A_GROUPS]
    d = {}
    d['x_prompt'] = nrm((BATCH, SEQ, D_MODEL), 1.0)
    d['x_sample'] = nrm((DEC_BATCH, DEC_SEQ, D_MODEL), 1.0)
    d['cache_a0'] = nrm((N_EVEN, DEC_BATCH, L[0], 2, A_HEADS_PER_GROUP, A_HEAD_DIM), 1.0)
    d['cache_a1'] = nrm((N_EVEN, DEC_BATCH, L[1], 2, A_HEADS_PER_GROUP, A_HEAD_DIM), 1.0)
    d['cache_a2'] = nrm((N_EVEN, DEC_BATCH, L[2], 2, A_HEADS_PER_GROUP, A_HEAD_DIM), 1.0)
    d['state_b_shift'] = nrm((N_EVEN, DEC_BATCH, B_COLS), 1.0)
    d['state_b_wkv'] = nrm((N_EVEN, DEC_BATCH, B_HEADS, B_HEAD_DIM, B_HEAD_DIM), 0.5)
    d['state_c'] = nrm((N_ODD, DEC_BATCH, C_HEADS, C_EXPAND, C_VDIM_HEAD), 0.5)
    d['rel_bias'] = nrm((N_BUCKETS, A_HEADS), 0.5)
    d['norm_mix'] = 1.0 + nrm((DEPTH, D_MODEL), 0.05)
    d['norm_mlp'] = 1.0 + nrm((DEPTH, D_MODEL), 0.05)
    d['norm_final'] = 1.0 + nrm((D_MODEL,), 0.05)
    d['e_w_in'] = nrm((N_EVEN, D_MODEL, E_COLS), D_MODEL ** -0.5)
    d['e_mu'] = jax.random.uniform(next(ks), (N_EVEN, B_COLS), jnp.float32)
    d['e_w0'] = nrm((N_EVEN, B_WIDTH), 0.5)
    d['e_w2'] = nrm((N_EVEN, DECAY_LORA, B_WIDTH), DECAY_LORA ** -0.5)
    d['e_a0'] = nrm((N_EVEN, B_WIDTH), 0.5)
    d['e_a2'] = nrm((N_EVEN, AAA_LORA, B_WIDTH), AAA_LORA ** -0.5)
    d['e_g2'] = nrm((N_EVEN, GATE_LORA, B_WIDTH), GATE_LORA ** -0.5)
    d['e_k_k'] = 0.85 + nrm((N_EVEN, B_WIDTH), 0.05)
    d['e_k_a'] = 1.0 + nrm((N_EVEN, B_WIDTH), 0.05)
    d['e_r_k'] = nrm((N_EVEN, B_HEADS, B_HEAD_DIM), 0.1)
    d['e_lnx_w'] = 1.0 + nrm((N_EVEN, B_WIDTH), 0.05)
    d['e_lnx_b'] = nrm((N_EVEN, B_WIDTH), 0.02)
    d['e_w_out'] = nrm((N_EVEN, MIX_WIDTH, D_MODEL), MIX_WIDTH ** -0.5)
    d['c_w_in'] = nrm((N_ODD, D_MODEL, C_COLS), D_MODEL ** -0.5)
    d['c_lb_raw'] = nrm((DEPTH, C_FDIM), 0.5)
    d['c_norm'] = 1.0 + nrm((N_ODD, D_MODEL), 0.05)
    d['c_w_out'] = nrm((N_ODD, D_MODEL, D_MODEL), D_MODEL ** -0.5)
    d['mlp_up'] = nrm((DEPTH, D_MODEL, D_FF), D_MODEL ** -0.5)
    d['mlp_down'] = nrm((DEPTH, D_FF, D_MODEL), D_FF ** -0.5)
    return d

def reference(x_prompt, x_sample, cache_a0, cache_a1, cache_a2, state_b_shift, state_b_wkv, state_c,
              rel_bias, norm_mix, norm_mlp, norm_final, e_w_in, e_mu, e_w0, e_w2, e_a0, e_a2, e_g2,
              e_k_k, e_k_a, e_r_k, e_lnx_w, e_lnx_b, e_w_out, c_w_in, c_lb_raw, c_norm, c_w_out,
              mlp_up, mlp_down):
    p = dict(rel_bias=rel_bias, norm_mix=norm_mix, norm_mlp=norm_mlp, norm_final=norm_final,
             e_w_in=e_w_in, e_mu=e_mu, e_w0=e_w0, e_w2=e_w2, e_a0=e_a0, e_a2=e_a2, e_g2=e_g2,
             e_k_k=e_k_k, e_k_a=e_k_a, e_r_k=e_r_k, e_lnx_w=e_lnx_w, e_lnx_b=e_lnx_b, e_w_out=e_w_out,
             c_w_in=c_w_in, c_lb_raw=c_lb_raw, c_norm=c_norm, c_w_out=c_w_out,
             mlp_up=mlp_up, mlp_down=mlp_down)
    dt = x_prompt.dtype
    bp = x_prompt.shape[0]
    p_fronts = [jnp.zeros((N_EVEN, bp, w, 2, A_HEADS_PER_GROUP, A_HEAD_DIM), dt) for w, _ in A_GROUPS]
    y_prompt, p_kv, p_shift, p_wkv, p_c = trunk(
        x_prompt, 0, p_fronts,
        jnp.zeros((N_EVEN, bp, B_COLS), jnp.float32),
        jnp.zeros((N_EVEN, bp, B_HEADS, B_HEAD_DIM, B_HEAD_DIM), jnp.float32),
        jnp.zeros((N_ODD, bp, C_HEADS, C_EXPAND, C_VDIM_HEAD), jnp.float32), p)
    s_fronts = [jnp.pad(c, ((0, 0), (0, 0), (w - c.shape[2], 0), (0, 0), (0, 0), (0, 0)))
                for c, (w, _) in zip((cache_a0, cache_a1, cache_a2), A_GROUPS)]
    y_sample, s_kv, s_shift, s_wkv, s_c = trunk(
        x_sample, PAST_LEN, s_fronts, state_b_shift, state_b_wkv, state_c, p)
    p_a0, p_a1, p_a2 = p_kv
    s_a0, s_a1, s_a2 = s_kv
    return (y_prompt, y_sample, p_a0, p_a1, p_a2, p_shift, p_wkv, p_c,
            s_a0, s_a1, s_a2, s_shift, s_wkv, s_c)


_drawn_inputs = setup_inputs


def setup_inputs(seed=0):
    import zlib

    import numpy as np

    out = dict(_drawn_inputs(seed))
    spreads = {}
    factors = {'e_k_k': 5.561, 'e_lnx_b': 4.414, 'c_norm': 3.403}
    for name, (base, spread) in spreads.items():
        noise = np.random.default_rng([zlib.crc32(name.encode()), seed]).standard_normal(out[name].shape)
        drawn = base * np.exp(spread * noise) if base else spread * noise
        out[name] = __import__('jax').numpy.asarray(drawn.astype(out[name].dtype))
    for name, factor in factors.items():
        out[name] = (out[name] * factor).astype(out[name].dtype)
    return out
```

```python
from contextlib import ExitStack, contextmanager

import numpy as np
import concourse.bass as bass
from concourse import mybir

F32 = mybir.dt.float32
F32R = mybir.dt.float32r
BF16 = mybir.dt.bfloat16
U8 = mybir.dt.uint8
ALU = mybir.AluOpType
ACT = mybir.ActivationFunctionType
AX = mybir.AxisListType

P = 128
D = 1024
KC = D // P
SEQ = 1024
NSEQ, DSEQ = 8, 4
NS = NSEQ * DSEQ
T = SEQ + NS
NT = 3
TC = T // NT
NB = SEQ // P
EPS = 1e-6


class Steps:

    def __init__(self, sem, known):
        self.sem, self.known, self.count = sem, known, 0
        self.base, self.inside = None, []

    def begin(self, engine, head_start=256):
        engine.sem_inc(self.sem, head_start)
        self.count = head_start

    def step(self, label=None):
        self.count += 1
        if label is not None:
            assert label not in self.inside or self.base is None, label
            if self.base is None:
                self.known[label] = (0, self.count, 0, 1)
            else:
                self.inside.append(label)
                self.known[label] = (self.base, self.count - self.base, self.known.get(label, (0, 0, 1, 1))[2],
                                     self.rounds)
        return 1

    @contextmanager
    def loop(self, engine, rounds, first=0):
        self.base, self.inside, self.rounds = self.count, [], rounds
        with engine.Fori(first, first + rounds) as i:
            yield i
        per = self.count - self.base
        for label in self.inside:
            base, place, _, _ = self.known[label]
            self.known[label] = (base, place, per, rounds)
        self.count = self.base + per * rounds
        self.base = None


class Plan:

    def __init__(self, nc, ctx, known):
        self.known = known
        self.passed = ctx.enter_context(nc.semaphore("passed"))
        self.steps = {name: Steps(ctx.enter_context(nc.semaphore(f"{name}_done")), known)
                      for name in ("pe", "act", "dve", "pool")}
        self.pe_done, self.act_done, self.dve_done, self.pool_done = (s.sem for s in self.steps.values())

    def value(self, label, i=None, lag=0):
        if label not in self.known:
            return 1
        base, place, per, rounds = self.known[label]
        if per == 0:
            return base + place
        if i is None:
            return base + (rounds - 1 - lag) * per + place
        if isinstance(i, int):
            return base + (i - lag) * per + place
        assert base + place - lag * per > 0 or base == 0, label
        return i * per + (base + place - lag * per)

    def sem(self, label):
        return self.steps[label.split(".")[0]].sem

    def before(self, label, i=None):
        return self.value(label, i) - 1 if label in self.known else 1

    def alone(self, engine, i):
        if i is not None and not isinstance(i, int):
            engine.sem_inc(self.passed, 1)

WIDE = T * 4
ACT_HI = 16512
ACT_LO = ACT_HI + KC * WIDE
W_SLOTS = 3
W_TILE = KC * P * 4
W_HI = ACT_LO + KC * WIDE
W_LO = W_HI + W_SLOTS * W_TILE
W_RAW = W_LO + W_SLOTS * W_TILE
CONST = W_RAW + W_TILE
ARENA = CONST + 9216
X_AT = 195552
LEVELS = [1, 2, 4, 8, 16, 32, 64]
DIAG, UPPER, UPPER_EQ, LOWER = 14, 15, 16, 17
VEC = {}
_n = 0
for _name, _cols in (("norm_mix0", KC), ("norm_mix1", KC), ("norm_mlp0", KC), ("norm_mlp1", KC), ("norm_final", KC),
                     ("c_norm", KC), ("lb0", KC), ("lb1", KC), ("mu", 21), ("w0", 6), ("a0", 6), ("k_k", 6),
                     ("k_a", 6), ("r_k", 6), ("lnx_w", 6), ("lnx_b", 6)):
    VEC[_name] = (_n, _cols)
    _n += _cols
NVEC = _n
TILES_A, TILES_LORA, TILES_B, TILES_OUT = 18, 3, 18, KC
FF_TILES = 32
TILES_MLP, TILES_C = 2 * FF_TILES, 32


class Kernel:

    def __init__(self, nc, ctx, io, known):
        self.nc, self.ctx, self.io = nc, ctx, io
        self.plan = Plan(nc, ctx, known)
        self.act_hi = self.at("act_hi", [P, KC, T], F32R, ACT_HI)
        self.act_lo = self.at("act_lo", [P, KC, T], F32R, ACT_LO)
        self.w_hi = self.at("w_hi", [P, W_SLOTS, KC, P], F32R, W_HI)
        self.w_lo = self.at("w_lo", [P, W_SLOTS, KC, P], F32R, W_LO)
        self.slots = [(self.w_hi[:, n], self.w_lo[:, n]) for n in range(W_SLOTS)]
        self.w_raw = self.at("w_raw", [P, KC * P], F32, W_RAW)
        o = CONST
        self.vec = self.at("vec", [P, NVEC], F32, o); o += 4 * NVEC
        self.derived = self.at("derived", [P, 64], F32, o); o += 256
        self.ident = self.at("ident", [P, P], F32, o); o += 512
        self.ones = self.at("ones", [P, P], F32, o); o += 512
        self.half_ones = self.at("half_ones", [P, P], F32, o); o += 512
        self.masks = self.at("masks", [P, 21, P], U8, o); o += 21 * P
        self.masks_in = self.at("masks_in", [P, 21, P], F32, ARENA)
        self.seq_mask = self.at("seq_mask", [NS, NSEQ], F32, o); o += NSEQ * 4
        self.ident2 = self.at("ident2", [P, 64], F32, o); o += 256
        self.last_rows = self.at("last_rows", [P, 9 * 21], F32, o); o += 9 * 21 * 4
        self.one_less_ka = self.at("one_less_ka", [P, 6], F32, o); o += 24
        self.shift = self.at("shift", [P, 8 * 21], F32, o); o += 8 * 21 * 4
        assert o <= ARENA, o - ARENA
        self.x = self.at("x", [P, KC, T], F32, X_AT)
        self.psum = ctx.enter_context(nc.psum_tensor("psum", [P, 8, 512], F32))
        self.dma_sems = {}
        self.pool_first = 256
        self.zeros = self.derived[:, 1:2].broadcast_to([P, KC * P])

    def at(self, name, shape, dtype, offset):
        size = {F32: 4, F32R: 4, BF16: 2, U8: 1}[dtype]
        for n in shape[1:]:
            size *= n
        assert offset % 4 == 0 and offset + size <= 229368, (name, offset + size - 229368)
        return self.nc.alloc_sbuf_tensor_at(name, shape, dtype, offset=offset, align_bytes=4)

    def sem(self, name):
        if name not in self.dma_sems:
            self.dma_sems[name] = self.ctx.enter_context(self.nc.semaphore(name))
        return self.dma_sems[name]

    def column(self, name, c, lo=0, hi=P):
        n = VEC[name][0] + c
        return self.vec[lo:hi, n:n + 1]

    def known_alias(self, name, label):
        self.plan.known[name] = self.plan.known[label]
        for s in self.plan.steps.values():
            if s.base is not None and label in s.inside:
                s.inside.append(name)

    def load_weight(self, sp, n, i=None):
        if not isinstance(n, int) or n > 0:
            sp.wait_ge(self.plan.steps["pool"].sem, n * 2 + self.pool_first)
        sp.dma_start(self.w_raw[:, :], self.io["weights"][bass.ds(n, 1)].rearrange("o p w -> (o p) w"))\
            .then_inc(self.sem("w_loaded"), 16)

    def split_weight(self, pool, n, slot, slots=None):
        plan = self.plan
        raw = self.w_raw[:, :]
        hi, lo = (w.rearrange("p k c -> p (k c)") for w in (slots or self.slots)[slot])
        pool.wait_ge(self.sem("w_loaded"), (n + 1) * 16)
        s = plan.steps["pool"]
        pool.tensor_tensor(hi, raw, self.zeros, ALU.add).then_inc(s.sem, s.step())
        pool.wait_ge(s.sem, n * 2 + self.pool_first + 1)
        pool.tensor_tensor(lo, raw, hi.bitcast(F32), ALU.subtract).then_inc(s.sem, s.step())

    def weight_ready(self, pe, n):
        pe.wait_ge(self.plan.steps["pool"].sem, (n + 1) * 2 + self.pool_first)

    def product(self, pe, slot, bank, c):
        out = self.psum[:, bank, 0:TC]
        cols = slice(c * TC, (c + 1) * TC)
        for k in range(KC):
            for m, (w, h) in enumerate(((self.w_hi, self.act_hi), (self.w_hi, self.act_lo), (self.w_lo, self.act_hi))):
                last = pe.matmul(out, w[:, slot, k, :], h[:, k, cols], start=(k == 0 and m == 0),
                                 stop=(k == KC - 1 and m == 2))
        return last

class Norm:
    def __init__(self, K, name, gain, ready, free):
        self.K, self.n, self.gain, self.ready, self.free = K, name, gain, ready, free
        a = Norm.scratch
        self.sq = K.at(f"{name}_sq", [P, 2, T], F32, a)
        self.acc = K.at(f"{name}_acc", [P, T], F32, a + 2 * WIDE)
        self.rstd = K.at(f"{name}_rstd", [P, NT, TC], F32, a + 3 * WIDE)
        self.h = K.at(f"{name}_h", [P, 4, TC], F32, a + 4 * WIDE)
        self.order = [(c, k) for c in range(NT) for k in range(KC)]

    scratch = ARENA

    def act(self, act):
        self.act_root(act)
        self.act_split(act)

    def act_root(self, act):
        K, n, plan = self.K, self.n, self.K.plan
        s = plan.steps["act"]
        for label in self.ready:
            act.wait_ge(plan.sem(label), plan.value(label))
        for k in range(KC):
            if k >= 2:
                act.wait_ge(plan.dve_done, plan.value(f"dve.{n}.acc{k - 2}"))
            act.activation(self.sq[:, k % 2], K.x[:, k], ACT.Square).then_inc(s.sem, s.step(f"act.{n}.sq{k}"))
        for c in range(NT):
            act.wait_ge(plan.pe_done, plan.value(f"pe.{n}.sum{c}"))
            act.activation(self.rstd[:, c], K.psum[:, c, 0:TC], ACT.Sqrt, bias=K.derived[:, 0:1],
                           scale=1.0 / D).then_inc(s.sem, s.step(f"act.{n}.rms{c}"))

    def act_split(self, act):
        K, n, plan = self.K, self.n, self.K.plan
        s = plan.steps["act"]
        for label in self.free:
            act.wait_ge(plan.sem(label), plan.value(label))
        for m, (c, k) in enumerate(self.order):
            act.wait_ge(plan.dve_done, plan.value(f"dve.{n}.h{m}"))
            act.activation(K.act_hi[:, k, c * TC:(c + 1) * TC], self.h[:, m % 4], ACT.Copy)\
                .then_inc(s.sem, s.step(f"act.{n}.hi{m}"))

    def dve(self, dve):
        self.dve_root(dve)
        self.dve_split(dve)

    def dve_root(self, dve):
        K, n, plan = self.K, self.n, self.K.plan
        s = plan.steps["dve"]
        for label in self.ready:
            dve.wait_ge(plan.sem(label), plan.value(label))
        for k in range(KC):
            dve.wait_ge(plan.act_done, plan.value(f"act.{n}.sq{k}"))
            if k == 0:
                dve.tensor_copy(self.acc[:], self.sq[:, 0]).then_inc(s.sem, s.step(f"dve.{n}.acc0"))
            else:
                dve.wait_ge(plan.dve_done, plan.value(f"dve.{n}.acc{k - 1}"))
                dve.tensor_tensor(self.acc[:], self.acc[:], self.sq[:, k % 2], ALU.add)\
                    .then_inc(s.sem, s.step(f"dve.{n}.acc{k}"))
        for c in range(NT):
            dve.wait_ge(plan.act_done, plan.value(f"act.{n}.rms{c}"))
            dve.reciprocal(self.rstd[:, c], self.rstd[:, c]).then_inc(s.sem, s.step(f"dve.{n}.rstd{c}"))

    def dve_split(self, dve):
        K, n, plan = self.K, self.n, self.K.plan
        s = plan.steps["dve"]

        def low(m):
            c, k = self.order[m]
            cols = slice(c * TC, (c + 1) * TC)
            dve.wait_ge(plan.act_done, plan.value(f"act.{n}.hi{m}"))
            dve.tensor_tensor(K.act_lo[:, k, cols], self.h[:, m % 4], K.act_hi[:, k, cols].bitcast(F32),
                              ALU.subtract).then_inc(s.sem, s.step(f"dve.{n}.lo{m}"))

        for label in self.free:
            dve.wait_ge(plan.sem(label), plan.value(label))
        for m, (c, k) in enumerate(self.order):
            dve.wait_ge(plan.dve_done, plan.value(f"dve.{n}.rstd{c}"))
            if m >= 4:
                dve.wait_ge(plan.dve_done, plan.value(f"dve.{n}.lo{m - 4}"))
            dve.scalar_tensor_tensor(out=self.h[:, m % 4], in0=K.x[:, k, c * TC:(c + 1) * TC],
                                     scalar=K.column(self.gain, k), in1=self.rstd[:, c],
                                     op0=ALU.mult, op1=ALU.mult).then_inc(s.sem, s.step(f"dve.{n}.h{m}"))
            if m >= 2:
                low(m - 2)
        low(len(self.order) - 2)
        low(len(self.order) - 1)

    def pe(self, pe):
        K, n, plan = self.K, self.n, self.K.plan
        pe.wait_ge(plan.dve_done, plan.value(f"dve.{n}.acc{KC - 1}"))
        for c in range(NT):
            pe.matmul(K.psum[:, c, 0:TC], K.ones[:, :], self.acc[:, c * TC:(c + 1) * TC],
                      start=True, stop=True).then_inc(plan.steps["pe"].sem, plan.steps["pe"].step(f"pe.{n}.sum{c}"))

    def wait_chunk(self, pe, c):
        pe.wait_ge(self.K.plan.dve_done, self.K.plan.value(f"dve.{self.n}.lo{KC * (c + 1) - 1}"))


class FinalNorm(Norm):

    def act(self, act):
        K, n, plan = self.K, self.n, self.K.plan
        self.act_root(act)
        for k in range(KC):
            act.wait_ge(plan.dve_done, plan.value(f"dve.{n}.y{k}"))
            act.dma_start(K.io["y"][:, k, :], self.sq[:, k % 2]).then_inc(K.sem(f"y_stored{k % 2}"), 16)
        for b in range(2):
            act.wait_ge(K.sem(f"y_stored{b}"), KC // 2 * 16)

    def dve(self, dve):
        K, n, plan = self.K, self.n, self.K.plan
        s = plan.steps["dve"]
        self.dve_root(dve)
        dve.wait_ge(plan.dve_done, plan.value(f"dve.{n}.rstd{NT - 1}"))
        for k in range(KC):
            if k >= 2:
                dve.wait_ge(K.sem(f"y_stored{k % 2}"), k // 2 * 16)
            dve.scalar_tensor_tensor(out=self.sq[:, k % 2], in0=K.x[:, k],
                                     scalar=K.column(self.gain, k),
                                     in1=self.rstd[:].rearrange("p c t -> p (c t)"),
                                     op0=ALU.mult, op1=ALU.mult).then_inc(s.sem, s.step(f"dve.{n}.y{k}"))


class MLP:

    GROUPS, RING, CHUNKS = FF_TILES // 2, 6, 30

    def __init__(self, K, name, w0, norm):
        self.K, self.n, self.w0, self.norm = K, name, w0, norm
        a = MLP.scratch
        self.u_hi = K.at(f"{name}_u_hi", [P, 4, T], F32R, a)
        self.u_lo = K.at(f"{name}_u_lo", [P, 4, T], F32R, a + 4 * WIDE)
        self.r = K.at(f"{name}_r", [P, 2, TC], F32, a + 8 * WIDE)
        self.u = K.at(f"{name}_u", [P, 2, TC], F32, a + 8 * WIDE + 2 * TC * 4)
        extra = a + 8 * WIDE + 4 * TC * 4
        self.slots = K.slots + [(K.at(f"{name}_w_hi", [P, KC, P], F32R, extra), K.at(f"{name}_w_lo", [P, KC, P], F32R, extra + W_TILE))]
        assert extra + 2 * W_TILE <= X_AT
        self.head = [("up", 0)]
        self.body = [("up", 1), ("down", 0), ("up", 0), ("down", 1)]
        self.tail = [("up", 1), ("down", 0), ("down", 1)]

    scratch = ARENA + 5 * WIDE + 64

    def parts(self):
        return (("head", self.head, 1), ("body", self.body, self.GROUPS // 2 - 1), ("tail", self.tail, 1))

    def chunks(self, section):
        out = []
        for p, (what, g) in enumerate(dict((s, l) for s, l, _ in self.parts())[section]):
            if what == "up":
                out += [f"act.{self.n}.{section}{p}.relu{j}.{c}" for j in range(2) for c in range(NT)]
            else:
                out += [f"dve.{self.n}.{section}{p}.add{k}.{c}" for k in range(KC) for c in range(NT)]
        return out

    def freed(self, section, m):
        mine = self.chunks(section)
        if m >= self.RING:
            return [(mine[m - self.RING], 0)]
        if section == "body":
            return [(mine[len(mine) + m - self.RING], 1), (self.chunks("head")[m], None)]
        if section == "tail":
            last = self.chunks("body")
            return [(last[len(last) + m - self.RING], None)]
        return []

    def walk(self, steps, engine, do):
        for section, parts, rounds in self.parts():
            def once(i):
                chunk = 0
                for p, (what, g) in enumerate(parts):
                    do(section, p, what, g, i, chunk)
                    chunk += 2 * NT if what == "up" else KC * NT
            if rounds > 1:
                with steps.loop(engine, rounds) as i:
                    once(i)
            else:
                once(None)

    def tile(self, section, p, i):
        if section == "head":
            return self.w0
        if section == "body":
            return i * 8 + (self.w0 + 2 + 2 * p)
        return self.w0 + 2 + 8 * (self.GROUPS // 2 - 1) + 2 * p

    def u_of(self, section, p, what, g):
        return g

    def up_before(self, section, p):
        return {("body", 1): ("body", 2, 1), ("body", 3): ("body", 0, 0),
                ("tail", 1): ("body", 2, None), ("tail", 2): ("tail", 0, 0)}[section, p]

    def down_before(self, section, p):
        return {("head", 0): None, ("body", 0): ("body", 3, 1), ("body", 2): ("body", 1, 0),
                ("tail", 0): ("body", 3, None)}[section, p]

    def pe(self, pe):
        K, n, plan = self.K, self.n, self.K.plan
        s = plan.steps["pe"]

        def do(section, p, what, g, i, chunk):
            tile = self.tile(section, p, i)
            w_hi, w_lo = zip(*self.slots[2 * self.pair(section, p):][:2])
            if section == "head":
                self.norm.wait_chunk(pe, NT - 1)
                pe.wait_ge(plan.dve_done, plan.value(f"dve.{self.norm.n}.lo{KC * NT - 1}"))
            if what == "up":
                for j in range(2):
                    K.weight_ready(pe, tile + j)
                    for c in range(NT):
                        m = chunk + NT * j + c
                        for label, lag in self.freed(section, m):
                            pe.wait_ge(plan.sem(label), plan.value(label, None if lag is None else i, lag or 0))
                            plan.alone(pe, None if lag is None else i)
                        out = K.psum[:, m % self.RING, 0:TC]
                        cols = slice(c * TC, (c + 1) * TC)
                        for k in range(KC):
                            for t, (w, h) in enumerate(((w_hi, K.act_hi), (w_hi, K.act_lo), (w_lo, K.act_hi))):
                                last = pe.matmul(out, w[j][:, k, :], h[:, k, cols], start=(k == 0 and t == 0),
                                                 stop=(k == KC - 1 and t == 2))
                        last.then_inc(s.sem, s.step(f"pe.{n}.{section}{p}.up{j}.{c}"))
            else:
                K.weight_ready(pe, tile + 1)
                us, up, lag = self.up_before(section, p)
                pe.wait_ge(plan.dve_done, plan.value(f"dve.{n}.{us}{up}.lo1.{NT - 1}", None if lag is None else i, lag or 0))
                plan.alone(pe, None if lag is None else i)
                if (section, p) == ("body", 1):
                    pe.wait_ge(plan.dve_done, plan.value(f"dve.{n}.head0.lo1.{NT - 1}"))
                for k in range(KC):
                    for c in range(NT):
                        m = chunk + NT * k + c
                        for label, lag in self.freed(section, m):
                            pe.wait_ge(plan.sem(label), plan.value(label, None if lag is None else i, lag or 0))
                            plan.alone(pe, None if lag is None else i)
                        out = K.psum[:, m % self.RING, 0:TC]
                        cols = slice(c * TC, (c + 1) * TC)
                        for j in range(2):
                            for t, (w, u) in enumerate(((w_hi, self.u_hi), (w_hi, self.u_lo), (w_lo, self.u_hi))):
                                last = pe.matmul(out, w[j][:, k, :], u[:, 2 * g + j, cols],
                                                 start=(j == 0 and t == 0), stop=(j == 1 and t == 2))
                        last.then_inc(s.sem, s.step(f"pe.{n}.{section}{p}.down{k}.{c}"))

        self.walk(s, pe, do)

    def act(self, act):
        K, n, plan = self.K, self.n, self.K.plan
        s = plan.steps["act"]

        def do(section, p, what, g, i, chunk):
            if what == "down":
                return
            before = self.down_before(section, p)
            if before:
                bs, bp, lag = before
                act.wait_ge(plan.pe_done, plan.value(f"pe.{n}.{bs}{bp}.down{KC - 1}.{NT - 1}", None if lag is None else i, lag or 0))
                plan.alone(act, None if lag is None else i)
            here = f"{n}.{section}{p}"

            def high(m):
                j, c = divmod(m, NT)
                act.wait_ge(plan.dve_done, plan.value(f"dve.{here}.u{j}.{c}", i))
                plan.alone(act, i)
                act.activation(self.u_hi[:, 2 * g + j, c * TC:(c + 1) * TC], self.u[:, m % 2], ACT.Copy)\
                    .then_inc(s.sem, s.step(f"act.{here}.hi{j}.{c}"))

            for m in range(2 * NT):
                j, c = divmod(m, NT)
                act.wait_ge(plan.pe_done, plan.value(f"pe.{here}.up{j}.{c}", i))
                plan.alone(act, i)
                if m >= 2:
                    act.wait_ge(plan.dve_done, plan.value(f"dve.{here}.u{(m - 2) // NT}.{(m - 2) % NT}", i))
                    plan.alone(act, i)
                act.activation(self.r[:, m % 2], K.psum[:, (chunk + m) % self.RING, 0:TC], ACT.Relu)\
                    .then_inc(s.sem, s.step(f"act.{here}.relu{j}.{c}"))
                if m >= 1:
                    high(m - 1)
            high(2 * NT - 1)

        self.walk(s, act, do)

    def dve(self, dve):
        K, n, plan = self.K, self.n, self.K.plan
        s = plan.steps["dve"]

        def do(section, p, what, g, i, chunk):
            here = f"{n}.{section}{p}"
            if what == "up":
                def low(m):
                    j, c = divmod(m, NT)
                    cols = slice(c * TC, (c + 1) * TC)
                    dve.wait_ge(plan.act_done, plan.value(f"act.{here}.hi{j}.{c}", i))
                    plan.alone(dve, i)
                    dve.tensor_tensor(self.u_lo[:, 2 * g + j, cols], self.u[:, m % 2],
                                      self.u_hi[:, 2 * g + j, cols].bitcast(F32), ALU.subtract)\
                        .then_inc(s.sem, s.step(f"dve.{here}.lo{j}.{c}"))
                for m in range(2 * NT):
                    j, c = divmod(m, NT)
                    dve.wait_ge(plan.act_done, plan.value(f"act.{here}.relu{j}.{c}", i))
                    plan.alone(dve, i)
                    if m >= 2:
                        dve.wait_ge(plan.dve_done, plan.value(f"dve.{here}.lo{(m - 2) // NT}.{(m - 2) % NT}", i))
                        plan.alone(dve, i)
                    elif m == 0:
                        dve.wait_ge(plan.dve_done, plan.before(f"dve.{here}.u0.0", i))
                        plan.alone(dve, i)
                    dve.tensor_tensor(self.u[:, m % 2], self.r[:, m % 2], self.r[:, m % 2], ALU.mult)\
                        .then_inc(s.sem, s.step(f"dve.{here}.u{j}.{c}"))
                    if m >= 1:
                        low(m - 1)
                low(2 * NT - 1)
            else:
                if section != "head":
                    for k in range(KC):
                        for c in range(NT):
                            dve.wait_ge(plan.pe_done, plan.value(f"pe.{here}.down{k}.{c}", i))
                            plan.alone(dve, i)
                            if (k, c) == (0, 0):
                                dve.wait_ge(plan.dve_done, plan.before(f"dve.{here}.add0.0", i))
                                plan.alone(dve, i)
                            cols = slice(c * TC, (c + 1) * TC)
                            dve.tensor_tensor(K.x[:, k, cols], K.x[:, k, cols],
                                              K.psum[:, (chunk + NT * k + c) % self.RING, 0:TC], ALU.add)\
                                .then_inc(s.sem, s.step(f"dve.{here}.add{k}.{c}"))

        self.walk(s, dve, do)

    def end(self):
        return [f"dve.{self.n}.tail2.add{KC - 1}.{NT - 1}"]

    def pe_end(self):
        return f"pe.{self.n}.tail2.down{KC - 1}.{NT - 1}"

    def pair(self, section, p):
        return 1 if section == "head" else p % 2

    def used(self, section, p, j, i):
        order = {("head", 0): [], ("body", 0): [("body", 2, 1)], ("body", 1): [("body", 3, 1), ("head", 0, None)],
                 ("body", 2): [("body", 0, 0)], ("body", 3): [("body", 1, 0)], ("tail", 0): [("body", 2, None)],
                 ("tail", 1): [("body", 3, None)], ("tail", 2): [("tail", 0, 0)]}[section, p]
        kinds = {s: l for s, l, _ in self.parts()}
        out = []
        for s, q, lag in order:
            what = kinds[s][q][0]
            label = f"pe.{self.n}.{s}{q}." + (f"up{j}.{NT - 1}" if what == "up" else f"down{KC - 1}.{NT - 1}")
            out.append((label, None if lag is None else i, lag or 0))
        return out

    def pool(self, pool, before):
        K = self.K

        def do(section, p, what, g, i, chunk):
            for j in range(2):
                for label, round, lag in self.used(section, p, j, i):
                    pool.wait_ge(K.plan.sem(label), K.plan.value(label, round, lag))
                    K.plan.alone(pool, round)
                if (section, p) == ("body", 0):
                    pool.wait_ge(K.plan.sem(before[j]), K.plan.value(before[j]))
                K.split_weight(pool, self.tile(section, p, i) + j, 2 * self.pair(section, p) + j, self.slots)

        self.walk(K.plan.steps["pool"], pool, do)

class Setup:

    def act(self, act, K):
        io, plan = K.io, K.plan
        s = plan.steps["act"]
        loaded = K.sem("constants_loaded")
        for dst, src in ((K.vec, "vec"), (K.ident, "ident"), (K.half_ones, "half_ones"), (K.masks_in, "masks"),
                         (K.seq_mask, "seq_mask"), (K.ident2, "ident2"),
                         (K.shift, "shift_in")):
            act.dma_start(dst[:], io[src]).then_inc(loaded, 16)
        act.wait_ge(plan.dve_done, plan.value("dve.setup.shift"))
        act.activation(K.derived[:, 32:48], K.derived[:, 32:48], ACT.Exp).then_inc(s.sem, s.step("act.setup.exp"))

    def dve(self, dve, K):
        plan = K.plan
        s = plan.steps["dve"]
        d = K.derived
        dve.memset(K.ones[:, :], 1.0).then_inc(s.sem, s.step())
        dve.memset(d[:, 0:1], EPS).then_inc(s.sem, s.step())
        dve.memset(d[:, 1:2], 0.0).then_inc(s.sem, s.step("dve.setup.zero"))
        dve.wait_ge(K.sem("constants_loaded"), 7 * 16)
        dve.tensor_copy(K.masks[:], K.masks_in[:]).then_inc(s.sem, s.step("dve.setup.masks"))
        lo, hi = (K.vec[:, VEC[n][0]:VEC[n][0] + KC] for n in ("lb0", "lb1"))
        dve.tensor_tensor(d[:, 48:56], lo, hi, ALU.max).then_inc(s.sem, s.step("dve.setup.max"))
        dve.wait_ge(plan.dve_done, plan.value("dve.setup.max"))
        dve.tensor_tensor(d[:, 32:40], lo, d[:, 48:56], ALU.subtract).then_inc(s.sem, s.step())
        dve.tensor_tensor(d[:, 40:48], hi, d[:, 48:56], ALU.subtract).then_inc(s.sem, s.step("dve.setup.shift"))
        dve.wait_ge(plan.act_done, plan.value("act.setup.exp"))
        dve.tensor_tensor(d[:, 48:56], d[:, 32:40], d[:, 40:48], ALU.add).then_inc(s.sem, s.step("dve.setup.sum"))
        dve.wait_ge(plan.dve_done, plan.value("dve.setup.sum"))
        dve.reciprocal(d[:, 56:64], d[:, 48:56]).then_inc(s.sem, s.step("dve.setup.rec"))
        dve.wait_ge(plan.dve_done, plan.value("dve.setup.rec"))
        dve.tensor_tensor(d[:, 8:16], d[:, 40:48], d[:, 56:64], ALU.mult).then_inc(s.sem, s.step("dve.setup.lb"))
        dve.wait_ge(plan.dve_done, plan.value("dve.setup.lb"))
        dve.tensor_scalar(d[:, 16:24], d[:, 8:16], -1.0, 1.0, ALU.mult, ALU.add)\
            .then_inc(s.sem, s.step("dve.setup.end"))

HEADS_A, HD, WINDOW = 4, 64, 128
DILATION = (1, 4, 16)
SCALE = HD ** -0.5
FAR = -1e30
ROW_A = HEADS_A * HD + 8
REL = 3 * P - 1


def unit(ap, u):
    return ap[:, u * P:(u + 1) * P]


class MixA:
    def __init__(self, K, w0, norm):
        self.K, self.w0, self.norm = K, w0, norm
        a = ARENA

        def take(name, shape, dtype=F32):
            nonlocal a
            t = K.at(f"a_{name}", shape, dtype, a)
            size = 4
            for n in shape[1:]:
                size *= n
            a += size
            return t
        self.qkv = take("qkv", [P, 6, T])
        self.vt = take("vt", [P, NB, HEADS_A * HD])
        self.bias = take("bias", [P, HEADS_A, 2 * P])
        self.s = take("s", [P, 2, HEADS_A, 2 * P])
        self.pT = take("pT", [P, 2, 2, HEADS_A, P])
        self.og = [take(f"og{g}", [P, NB, ROW_A]) for g in range(3)]
        self.w = take("w", [P, 3, NB * HEADS_A])
        self.rel = take("rel", [4, 3, REL])
        self.onehot = take("onehot", [32, 3, REL])
        self.rel_in = take("rel_in", [32, 12])
        self.rows = take("rows", [NS, 3, 3, 2 * P])
        assert a <= 229368, a - 229368
        self.mixT = K.at("a_mixT", [P, 2, SEQ], F32, ARENA)

    def halves(self, g, u):
        return (0, 1) if (g == 0 and u > 0) or (g == 1 and u % 2) else (1,)

    def bias_pe(self, pe):
        K, plan = self.K, self.K.plan
        pe.wait_ge(K.sem("rel_loaded"), 48)
        for g in range(3):
            last = pe.matmul(K.psum[0:4, 3 + g, 0:REL], self.rel_in[:, 4 * g:4 * g + 4], self.onehot[:, g],
                             start=True, stop=True)
        last.then_inc(plan.steps["pe"].sem, plan.steps["pe"].step("pe.A.rel"))

    def bias_dve(self, dve):
        K, plan = self.K, self.K.plan
        dve.wait_ge(plan.pe_done, plan.value("pe.A.rel"))
        dve.wait_ge(K.sem("rel_loaded"), 48)
        for g in range(3):
            dve.tensor_tensor(self.rel[:, g], self.rel[:, g], K.psum[0:4, 3 + g, 0:REL], ALU.add)\
                .then_inc(plan.steps["dve"].sem, plan.steps["dve"].step(f"dve.A.rel{g}"))

    def bias_act(self, act):
        K, plan = self.K, self.K.plan
        loaded = K.sem("rel_loaded")
        act.dma_start(self.rel_in[:], K.io["rel_bias"]).then_inc(loaded, 16)
        act.dma_start(self.onehot[:], K.io["onehot"]).then_inc(loaded, 16)
        act.dma_start(self.rel[:], K.io["outside"]).then_inc(loaded, 16)
        act.wait_ge(plan.dve_done, plan.value("dve.A.rel2"))
        act.dma_start(K.io["rel_rows"].rearrange("g h m -> h g m"), self.rel[:]).then_inc(K.sem("rel_stored"), 16)
        act.wait_ge(K.sem("rel_stored"), 16)
        rel, rows = K.io["rel_rows"], K.io["bias_rows"]
        act.dma_start(bass.AP(rows.tensor, rows.offset, [[4 * REL, P], [P * 4 * REL, 3], [1, 4 * REL]]),
                      bass.AP(rel.tensor, rel.offset, [[0, P], [4 * REL, 3], [1, 4 * REL]])).then_inc(K.sem("rel_stored"), 16)

    def bias_load(self, act, g):
        K = self.K
        rows = K.io["bias_rows"]
        src = bass.AP(rows.tensor, rows.offset + g * P * 4 * REL + P - 1,
                      [[4 * REL - 1, P], [REL, HEADS_A], [1, 2 * P]])
        act.dma_start(self.bias[:], src).then_inc(K.sem("bias_loaded"), 16)

    def pe(self, pe):
        K, plan, ps = self.K, self.K.plan, self.K.psum
        s = plan.steps["pe"]
        for g in range(3):
            for n in range(6):
                w = 6 * g + n
                K.weight_ready(pe, self.w0 + w)
                for c in range(NT):
                    if n:
                        pe.wait_ge(plan.act_done, plan.value(f"act.A{g}.in{n - 1}.{c}"))
                    elif g:
                        pe.wait_ge(plan.act_done, plan.value(f"act.A{g - 1}.in5.{c}"))
                    K.product(pe, (w + 1) % 2, c, c).then_inc(s.sem, s.step(f"pe.A{g}.in{n}.{c}"))
            for u in range(0, NB, 2):
                b = 3 + u // 2 % 2
                pe.wait_ge(plan.act_done, plan.value(f"act.A{g}.in5.{NT - 1}"))
                if u >= 4:
                    pe.wait_ge(plan.act_done, plan.value(f"act.A{g}.vt{u - 4}"))
                elif g:
                    pe.wait_ge(plan.act_done, plan.value(f"act.A{g - 1}.o{NB - 1}"))
                for k in range(2):
                    for n in range(2):
                        last = pe.transpose(ps[:, b, (2 * k + n) * P:(2 * k + n + 1) * P],
                                            unit(self.qkv[:, 4 + n], u + k), K.ident[:, :])
                last.then_inc(s.sem, s.step(f"pe.A{g}.vt{u}"))
            for kind in range(3):
                b = 5 + kind % 2
                if kind == 2:
                    pe.wait_ge(plan.act_done, plan.value(f"act.A{g}.row0"))
                elif g:
                    pe.wait_ge(plan.act_done, plan.value(f"act.A{g - 1}.pT{NB - 1}"))
                for n in range(2):
                    last = pe.transpose(ps[0:NS, b, n * P:(n + 1) * P], self.qkv[:, 2 * kind + n, SEQ:T], K.ident[:, :])
                last.then_inc(s.sem, s.step(f"pe.A{g}.row{kind}"))

            def scores(u):
                if u == 0:
                    pe.wait_ge(plan.act_done, plan.value(f"act.A{g}.vt{NB - 2}"))
                else:
                    pe.wait_ge(plan.dve_done, plan.value(f"dve.A{g}.s{u - 1}.1"))
                for h in range(HEADS_A):
                    r = slice(64 * (h % 2), 64 * (h % 2) + 64)
                    q = unit(self.qkv[r, h // 2], u)
                    for half in self.halves(g, u):
                        k = unit(self.qkv[r, 2 + h // 2], u - 1 + half)
                        out = ps[:, 3 + h % 2, (2 * (h // 2) + half) * P:(2 * (h // 2) + half + 1) * P]
                        last = pe.matmul(out, q, k, start=True, stop=True)
                last.then_inc(s.sem, s.step(f"pe.A{g}.s{u}"))

            def turn(u):
                pe.wait_ge(plan.act_done, plan.value(f"act.A{g}.p{u}"))
                if u:
                    pe.wait_ge(plan.act_done, plan.value(f"act.A{g}.pT{u - 1}"))
                else:
                    pe.wait_ge(plan.act_done, plan.value(f"act.A{g}.row2"))
                for half in self.halves(g, u):
                    for h in range(HEADS_A):
                        last = pe.transpose(ps[:, 5 + half, h * P:(h + 1) * P],
                                            self.s[:, u % 2, h, half * P:(half + 1) * P], K.ident[:, :])
                last.then_inc(s.sem, s.step(f"pe.A{g}.pT{u}"))

            def values(u):
                pe.wait_ge(plan.act_done, plan.value(f"act.A{g}.pT{u}"))
                if u:
                    pe.wait_ge(plan.act_done, plan.value(f"act.A{g}.o{u - 1}"))
                for h in range(HEADS_A):
                    hs = self.halves(g, u)
                    for half in hs:
                        last = pe.matmul(ps[:, 7, h * HD:(h + 1) * HD], self.pT[:, u % 2, half, h],
                                         self.vt[:, u - 1 + half, h * HD:(h + 1) * HD], start=(half == hs[0]),
                                         stop=(half == 1))
                last.then_inc(s.sem, s.step(f"pe.A{g}.o{u}"))

            scores(0)
            for u in range(NB):
                if u + 1 < NB:
                    scores(u + 1)
                turn(u)
                values(u)
        for b in range(NB):
            pe.wait_ge(plan.dve_done, plan.value(f"dve.A.out{b // 4}"))
            bank = 3 + b % 4
            if b >= 4:
                pe.wait_ge(plan.act_done, plan.value(f"act.A.mix{b - 4}"))
            else:
                pe.wait_ge(plan.act_done, plan.value(f"act.A2.o{NB - 1}"))
            for n in range(2):
                last = pe.transpose(ps[:, bank, n * P:(n + 1) * P], self.og[0][:, b, n * P:(n + 1) * P], K.ident[:, :])
            last.then_inc(s.sem, s.step(f"pe.A.mix{b}"))

    def act(self, act):
        K, plan, ps = self.K, self.K.plan, self.K.psum
        s = plan.steps["act"]
        for g in range(3):
            if g:
                act.wait_ge(plan.dve_done, plan.value(f"dve.A{g - 1}.s{NB - 1}.1"))
                act.wait_ge(K.sem("kv_stored"), 64 * g)
            else:
                act.wait_ge(K.sem("rel_stored"), 32)
            self.bias_load(act, g)
            for n in range(6):
                for c in range(NT):
                    act.wait_ge(plan.pe_done, plan.value(f"pe.A{g}.in{n}.{c}"))
                    if g and (n, c) == (0, 0):
                        act.wait_ge(plan.pe_done, plan.value(f"pe.A{g - 1}.s{NB - 1}"))
                    r, prompt = DILATION[g], min(SEQ - c * TC, TC)
                    dst = self.qkv[:, n, 0:SEQ].rearrange("p (c i) -> p i c", c=r)[:, c * TC // r:(c * TC + prompt) // r]
                    ins = act.activation(dst, ps[:, c, 0:prompt].rearrange("p (i c) -> p i c", c=r), ACT.Copy)
                    if prompt < TC:
                        ins = act.activation(self.qkv[:, n, SEQ:T], ps[:, c, prompt:TC], ACT.Copy)
                    ins.then_inc(s.sem, s.step(f"act.A{g}.in{n}.{c}"))
                if n >= 2:
                    act.wait_ge(plan.act_done, plan.value(f"act.A{g}.in{n}.{NT - 1}"))
                    act.dma_start(K.io["kv"][g, n - 2], self.qkv[:, n]).then_inc(K.sem("kv_stored"), 16)
            if g:
                act.wait_ge(plan.pe_done, plan.value(f"pe.A{g - 1}.o{NB - 1}"))
            for u in range(0, NB, 2):
                act.wait_ge(plan.pe_done, plan.value(f"pe.A{g}.vt{u}"))
                act.activation(flat(self.vt[:, u:u + 2]), ps[:, 3 + u // 2 % 2, :], ACT.Copy)\
                    .then_inc(s.sem, s.step(f"act.A{g}.vt{u}"))
            for kind in range(3):
                act.wait_ge(plan.pe_done, plan.value(f"pe.A{g}.row{kind}"))
                act.activation(self.rows[:, kind, g], ps[0:NS, 5 + kind % 2, 0:2 * P], ACT.Copy)\
                    .then_inc(s.sem, s.step(f"act.A{g}.row{kind}"))
            og = self.og[g]
            if g == 2:
                act.wait_ge(K.sem("og_stored"), 16)

            def weigh(u):
                act.wait_ge(plan.dve_done, plan.value(f"dve.A{g}.max{u}"))
                x = slice(P * self.halves(g, u)[0], 2 * P)
                for h in range(HEADS_A):
                    ins = act.activation(self.s[:, u % 2, h, x], self.s[:, u % 2, h, x], ACT.Exp,
                                         bias=og[:, u, 260 + h:261 + h], accum_out=og[:, u, 256 + h:257 + h])
                ins.then_inc(s.sem, s.step(f"act.A{g}.p{u}"))

            def turned(u):
                act.wait_ge(plan.pe_done, plan.value(f"pe.A{g}.pT{u}"))
                for half in self.halves(g, u):
                    ins = act.activation(self.pT[:, u % 2, half].rearrange("p h q -> p (h q)"), ps[:, 5 + half, :], ACT.Copy)
                ins.then_inc(s.sem, s.step(f"act.A{g}.pT{u}"))
                act.wait_ge(plan.pe_done, plan.value(f"pe.A{g}.o{u}"))
                act.activation(og[:, u, 0:256], ps[:, 7, 0:256], ACT.Copy).then_inc(s.sem, s.step(f"act.A{g}.o{u}"))

            weigh(0)
            for u in range(NB):
                if u + 1 < NB:
                    weigh(u + 1)
                turned(u)
            act.wait_ge(plan.act_done, plan.value(f"act.A{g}.o{NB - 1}"))
            rows = K.io["og_rows"]
            if g == 1:
                act.dma_start(rows[0].rearrange("(b i r) w -> i r b w", b=2, r=4),
                              og[:].rearrange("p (r b) w -> p r b w", b=2)).then_inc(K.sem("og_stored"), 16)
            if g == 2:
                for half in range(2):
                    act.dma_start(rows[1].rearrange("(i u h) w -> h i u w", u=NB, h=2)[half],
                                  og[64 * half:64 * half + 64]).then_inc(K.sem("og_stored"), 16)
        act.dma_start(K.io["rows"].rearrange("k g t w -> t k g w"), self.rows[:]).then_inc(K.sem("rows_stored"), 16)
        act.wait_ge(K.sem("og_stored"), 48)
        for g in (1, 2):
            act.dma_start(self.og[g][:], K.io["og_rows"][g - 1].rearrange("(b p) w -> p b w", p=P))\
                .then_inc(K.sem("og_loaded"), 16)
        act.wait_ge(plan.dve_done, plan.value("dve.A.shift"))
        act.activation(flat(self.w[:]), flat(self.w[:]), ACT.Exp).then_inc(s.sem, s.step("act.A.w"))
        act.wait_ge(K.sem("kv_stored"), 192)
        for b in range(NB):
            act.wait_ge(plan.pe_done, plan.value(f"pe.A.mix{b}"))
            act.activation(self.mixT[:, :, b * P:(b + 1) * P],
                           ps[:, 3 + b % 4, 0:2 * P].rearrange("p (n t) -> p n t", n=2), ACT.Copy)\
                .then_inc(s.sem, s.step(f"act.A.mix{b}"))
        act.wait_ge(plan.act_done, plan.value(f"act.A.mix{NB - 1}"))
        act.dma_start(K.io["mix"][0:2, :, 0:SEQ].rearrange("n p t -> p n t"), self.mixT[:]).then_inc(K.sem("a_mix_stored"), 16)
        act.wait_ge(K.sem("rows_stored"), 16)
        act.wait_ge(K.sem("a_mix_stored"), 16)

    def dve(self, dve):
        K, plan, ps = self.K, self.K.plan, self.K.psum
        s = plan.steps["dve"]
        for g in range(3):
            og = self.og[g]
            dve.wait_ge(K.sem("bias_loaded"), 16 * (g + 1))
            if g == 2:
                dve.memset(self.bias[64:P, :, P:P + 64], FAR).then_inc(s.sem, s.step("dve.A2.cut"))
                dve.wait_ge(plan.dve_done, plan.value("dve.A2.cut"))
            for u in range(NB):
                x = slice(P * self.halves(g, u)[0], 2 * P)
                dve.wait_ge(plan.pe_done, plan.value(f"pe.A{g}.s{u}"))
                if u >= 2:
                    dve.wait_ge(plan.pe_done, plan.value(f"pe.A{g}.pT{u - 2}"))
                elif g:
                    dve.wait_ge(plan.pe_done, plan.value(f"pe.A{g - 1}.pT{NB - 2 + u}"))
                for n in range(2):
                    dve.scalar_tensor_tensor(
                 out=self.s[:, u % 2, n::2, x],
                 in0=ps[:, 3 + n, :].rearrange("p (h x) -> p h x", h=2)[:, :, x], scalar=SCALE,
                 in1=self.bias[:, n::2, x], op0=ALU.mult, op1=ALU.add).then_inc(s.sem, s.step(f"dve.A{g}.s{u}.{n}"))
                dve.wait_ge(plan.dve_done, plan.value(f"dve.A{g}.s{u}.1"))
                dve.tensor_reduce(og[:, u, 260:264], self.s[:, u % 2, :, x], AX.X, ALU.max, negate=True)\
                    .then_inc(s.sem, s.step(f"dve.A{g}.max{u}"))
        dve.wait_ge(K.sem("og_loaded"), 32)
        dve.wait_ge(plan.act_done, plan.value(f"act.A0.o{NB - 1}"))
        m = [self.og[g][:, :, 260:264] for g in range(3)]
        l = [self.og[g][:, :, 256:260] for g in range(3)]
        w = [self.w[:, g].rearrange("p (b h) -> p b h", h=HEADS_A) for g in range(3)]

        def op(instruction, name):
            instruction.then_inc(s.sem, s.step(f"dve.A.{name}"))
            dve.wait_ge(plan.dve_done, plan.value(f"dve.A.{name}"))
        op(dve.tensor_tensor(w[0], m[0], m[1], ALU.min), "min0")
        op(dve.tensor_tensor(w[0], w[0], m[2], ALU.min), "min1")
        dve.tensor_tensor(w[1], w[0], m[1], ALU.subtract).then_inc(s.sem, s.step())
        op(dve.tensor_tensor(w[2], w[0], m[2], ALU.subtract), "shift2")
        dve.tensor_tensor(w[0], w[0], m[0], ALU.subtract).then_inc(s.sem, s.step("dve.A.shift"))
        dve.wait_ge(plan.act_done, plan.value("act.A.w"))
        for g in range(3):
            op(dve.tensor_tensor(l[g], l[g], w[g], ALU.mult), f"l{g}")
        op(dve.tensor_tensor(l[0], l[0], l[1], ALU.add), "den0")
        op(dve.tensor_tensor(l[0], l[0], l[2], ALU.add), "den1")
        op(dve.reciprocal(l[1], l[0]), "den")
        for g in range(3):
            op(dve.tensor_tensor(w[g], w[g], l[1], ALU.mult), f"wd{g}")
        for part in range(2):
            b = slice(4 * part, 4 * part + 4)
            for g in range(3):
                o = self.og[g][:, b, 0:256].rearrange("p b (h x) -> p b h x", h=HEADS_A)
                wg = self.w[:, g].rearrange("p (b h) -> p b h", h=HEADS_A)[:, b].unsqueeze(3).broadcast_to([P, 4, HEADS_A, HD])
                op(dve.tensor_tensor(o, o, wg, ALU.mult), f"o{part}{g}")
            o = [self.og[g][:, b, 0:256] for g in range(3)]
            op(dve.tensor_tensor(o[0], o[0], o[1], ALU.add), f"sum{part}")
            dve.tensor_tensor(o[0], o[0], o[2], ALU.add).then_inc(s.sem, s.step(f"dve.A.out{part}"))

    def pool(self, pool):
        K = self.K
        for w in range(TILES_A):
            if w >= 2:
                pool.wait_ge(K.plan.pe_done, K.plan.value(f"pe.A{(w - 2) // 6}.in{(w - 2) % 6}.{NT - 1}"))
            K.split_weight(pool, self.w0 + w, (w + 1) % 2)


class SampleA:

    CACHE = (0, 1, 5)
    NEW = 6

    def __init__(self, K):
        self.K = K
        a = ARENA

        def take(name, shape, dtype=F32):
            nonlocal a
            t = K.at(f"s_{name}", shape, dtype, a)
            size = 4
            for n in shape[1:]:
                size *= n
            a += size
            return t
        H = HEADS_A * HD
        self.cache = take("cache", [P, 2, 9, H])
        self.q = take("q", [P, 2, 3, DSEQ, H])
        self.prod = take("prod", [P, 3, DSEQ, H])
        self.sc = take("sc", [P, 3, P])
        self.st = take("st", [P, 3, P + DSEQ])
        self.bias = take("bias", [P, 3, P + DSEQ])
        self.pT = take("pT", [P, 3, P])
        self.qn = take("qn", [P, 3, HD])
        self.kn = take("kn", [P, self.NEW, HD])
        self.vn = take("vn", [P, self.NEW, HD])
        self.tmp = take("tmp", [P, self.NEW, HD])
        self.dots = take("dots", [P, 8])
        self.on = take("on", [P, 2, HD])
        self.small = take("small", [P, 8])
        self.of = take("of", [P, 2, NS])
        assert a <= 229368

    def source(self, q, part):
        io = self.K.io
        cut = slice(256 * part, 256 * part + 256)
        return ((self.CACHE[0], 1, io["cache_a0"][q].rearrange("(i o) w -> i o w", o=1)[:, :, cut]),
                (self.CACHE[1], 4, io["cache_a1"][q].rearrange("(i o) w -> i o w", o=4)[:, :, cut]),
                (self.CACHE[2], 4, io["cache_a2"][q].rearrange("(i o) w -> i o w", o=16)[:, 0:4, cut]))

    def load(self, engine, q, part):
        K = self.K
        n = part * NSEQ + q
        for at, count, src in self.source(q, part):
            engine.dma_start(self.cache[:, n % 2, at:at + count], src).then_inc(K.sem(f"cache_loaded{n % 2}"), 16)
        if part == 0:
            rows = K.io["rows"]
            src = bass.AP(rows.tensor, rows.offset + q * DSEQ * 256, [[0, P], [NS * 256, 3], [1, DSEQ * 256]])
            engine.dma_start(self.q[:, n % 2].rearrange("p g t x -> p g (t x)"), src)\
                .then_inc(K.sem(f"cache_loaded{n % 2}"), 16)

    def arrived(self, n):
        keys = min(n // 2 + 1, NSEQ // 2)
        return 16 * (4 * keys + 3 * max(0, n // 2 + 1 - NSEQ // 2))

    def act(self, act):
        K, plan, ps = self.K, self.K.plan, self.K.psum
        s = plan.steps["act"]
        io = K.io
        rows, rel = io["rows"], io["bias_rows"]
        new = K.sem("new_loaded")
        self.load(act, 0, 0)
        self.load(act, 1, 0)
        for g in range(3):
            act.dma_start(self.qn[:, g], rows[0, g].rearrange("t (h x) -> (t h) x", h=HEADS_A)).then_inc(new, 16)
        for kind, dst in ((1, self.kn), (2, self.vn)):
            base = rows.offset + kind * 3 * NS * 256
            for q in range(NSEQ):
                for t in range(DSEQ):
                    act.dma_start(dst[16 * q + 4 * t:16 * q + 4 * t + 4, 0:4],
                                  bass.AP(rows.tensor, base + q * DSEQ * 256, [[HD, HEADS_A], [256, DSEQ], [1, HD]]))\
                        .then_inc(new, 16)
            for g in (1, 2):
                act.dma_start(dst[:, 3 + g], rows[kind, g].rearrange("t (h x) -> (t h) x", h=HEADS_A)).then_inc(new, 16)
        for q in range(NSEQ):
            for g in range(3):
                width = P + DSEQ if g == 0 else P + 1
                act.dma_start(self.bias[16 * q:16 * q + 16, g, 0:width],
                              bass.AP(rel.tensor, rel.offset + g * P * 4 * REL + P - 1,
                                      [[4 * REL - (g == 0), DSEQ], [REL, HEADS_A], [1, width]])).then_inc(new, 16)
        for q in range(2, NSEQ):
            act.wait_ge(plan.dve_done, plan.value(f"dve.S.prod{q - 2}"))
            self.load(act, q, 0)
        for q in range(2):
            act.wait_ge(plan.dve_done, plan.value(f"dve.S.prod{NSEQ - 2 + q}"))
            self.load(act, q, 1)
        act.wait_ge(plan.dve_done, plan.value("dve.S.max"))
        act.activation(self.st[:].rearrange("p g x -> p (g x)"), self.st[:].rearrange("p g x -> p (g x)"), ACT.Exp,
                       bias=self.small[:, 0:1], accum_out=self.small[:, 1:2]).then_inc(s.sem, s.step("act.S.exp"))
        for q in range(2, NSEQ):
            act.wait_ge(plan.pe_done, plan.value(f"pe.S.o{q - 2}"))
            self.load(act, q, 1)
        act.wait_ge(plan.dve_done, plan.value("dve.S.of"))
        act.dma_start(io["mix"][0:2, :, SEQ:T].rearrange("n p t -> p n t"), self.of[:]).then_inc(K.sem("s_mix_stored"), 16)
        act.wait_ge(K.sem("s_mix_stored"), 16)

    def dve(self, dve):
        K, plan, ps = self.K, self.K.plan, self.K.psum
        s = plan.steps["dve"]

        def op(instruction, name):
            instruction.then_inc(s.sem, s.step(f"dve.S.{name}"))
            dve.wait_ge(plan.dve_done, plan.value(f"dve.S.{name}"))
        dve.wait_ge(K.sem("a_mix_stored"), 16)
        dve.wait_ge(plan.act_done, plan.value(f"act.A.mix{NB - 1}"))
        dve.memset(self.st[:, 1:3, P + 1:], FAR).then_inc(s.sem, s.step("dve.S.far"))
        for q in range(NSEQ):
            dve.wait_ge(K.sem(f"cache_loaded{q % 2}"), self.arrived(q))
            if q == 0:
                dve.wait_ge(plan.dve_done, plan.value("dve.S.far"))
            c = self.cache[:, q % 2]
            dve.tensor_tensor(self.prod[:, 0], c[:, 0:1].broadcast_to([P, DSEQ, 256]), self.q[:, q % 2, 0], ALU.mult)\
                .then_inc(s.sem, s.step())
            dve.tensor_tensor(self.prod[:, 1:3].rearrange("p g t x -> p (g t) x"), c[:, 1:9],
                              self.q[:, q % 2, 1:3].rearrange("p g t x -> p (g t) x"), ALU.mult)\
                .then_inc(s.sem, s.step(f"dve.S.prod{q}"))
            dve.wait_ge(plan.dve_done, plan.value(f"dve.S.prod{q}"))
            for g in range(3):
                dve.tensor_reduce(self.sc[:, g, 16 * q:16 * q + 16],
                                  self.prod[:, g].rearrange("p t (h x) -> p (t h) x", h=HEADS_A), AX.X, ALU.add)\
                    .then_inc(s.sem, s.step(f"dve.S.sc{q}.{g}"))
            dve.wait_ge(plan.dve_done, plan.value(f"dve.S.sc{q}.2"))
        dve.wait_ge(K.sem("new_loaded"), 16 * (3 + 2 * (NS + 2) + 3 * NSEQ))
        dve.tensor_tensor(self.tmp[:, 0:4], self.kn[:, 0:4], self.qn[:, 0:1].broadcast_to([P, 4, HD]), ALU.mult)\
            .then_inc(s.sem, s.step())
        op(dve.tensor_tensor(self.tmp[:, 4:6], self.kn[:, 4:6], self.qn[:, 1:3], ALU.mult), "tmp")
        op(dve.tensor_reduce(self.dots[:, 0:6], self.tmp[:], AX.X, ALU.add), "dots")
        dve.scalar_tensor_tensor(out=self.st[:, 0, P:], in0=self.dots[:, 0:4], scalar=SCALE,
                                 in1=self.bias[:, 0, P:], op0=ALU.mult, op1=ALU.add).then_inc(s.sem, s.step())
        dve.scalar_tensor_tensor(out=self.st[:, 1:3, P], in0=self.dots[:, 4:6], scalar=SCALE,
                                 in1=self.bias[:, 1:3, P], op0=ALU.mult, op1=ALU.add).then_inc(s.sem, s.step())
        dve.wait_ge(plan.pe_done, plan.value("pe.S.turn"))
        op(dve.scalar_tensor_tensor(out=self.st[:, :, 0:P], in0=ps[:, 3, 0:3 * P].rearrange("p (g x) -> p g x", g=3),
                                    scalar=SCALE, in1=self.bias[:, :, 0:P], op0=ALU.mult, op1=ALU.add), "st")
        whole = self.st[:].rearrange("p g x -> p (g x)")
        dve.tensor_reduce(self.small[:, 0:1], whole, AX.X, ALU.max, negate=True).then_inc(s.sem, s.step("dve.S.max"))
        dve.wait_ge(plan.act_done, plan.value("act.S.exp"))
        op(dve.reciprocal(self.small[:, 2:3], self.small[:, 1:2]), "rden")
        op(dve.tensor_scalar(whole, whole, self.small[:, 2:3], None, ALU.mult), "p")
        where = [(0, P), (0, P + 1), (0, P + 2), (0, P + 3), (1, P), (2, P)]
        for n, (g, x) in enumerate(where):
            w = self.st[:, g, x:x + 1]
            if n == 0:
                op(dve.tensor_scalar(self.on[:, 0], self.vn[:, 0], w, None, ALU.mult), "on0")
            else:
                op(dve.scalar_tensor_tensor(out=self.on[:, 0], in0=self.vn[:, n], scalar=w, in1=self.on[:, 0],
                                            op0=ALU.mult, op1=ALU.add), f"on{n}")
        dve.tensor_copy(self.on[:, 1], self.on[:, 0]).then_inc(s.sem, s.step("dve.S.on"))
        dve.wait_ge(plan.pe_done, plan.value("pe.S.turn_p"))
        dve.tensor_copy(flat(self.pT[:]), ps[:, 4, 0:3 * P]).then_inc(s.sem, s.step("dve.S.pT"))
        dve.wait_ge(plan.pe_done, plan.value(f"pe.S.o{NSEQ - 1}"))
        dve.wait_ge(plan.pe_done, plan.value("pe.S.turn_o"))
        for e in range(2):
            h = slice(64 * e, 64 * e + 64)
            dve.tensor_copy(self.of[h], ps[h, 5, 0:4 * NS].rearrange("p (t n e) -> p e n t", n=2, e=2)[:, e])\
                .then_inc(s.sem, s.step(f"dve.S.take{e}"))
        dve.wait_ge(plan.dve_done, plan.value("dve.S.take1"))
        for e in range(2):
            h = slice(64 * e, 64 * e + 64)
            dve.tensor_tensor(self.of[h], self.of[h],
                              ps[h, 6, 0:P].rearrange("p (t n e) -> p e n t", n=2, e=2)[:, e], ALU.add)\
                .then_inc(s.sem, s.step("dve.S.of" if e else None))

    def pe(self, pe):
        K, plan, ps = self.K, self.K.plan, self.K.psum
        s = plan.steps["pe"]
        pe.wait_ge(plan.dve_done, plan.value(f"dve.S.sc{NSEQ - 1}.2"))
        for g in range(3):
            last = pe.transpose(ps[:, 3, g * P:(g + 1) * P], self.sc[:, g], K.ident[:, :])
        last.then_inc(s.sem, s.step("pe.S.turn"))
        pe.wait_ge(plan.dve_done, plan.value("dve.S.p"))
        for g in range(3):
            last = pe.transpose(ps[:, 4, g * P:(g + 1) * P], self.st[:, g, 0:P], K.ident[:, :])
        last.then_inc(s.sem, s.step("pe.S.turn_p"))
        pe.wait_ge(plan.dve_done, plan.value("dve.S.on"))
        pe.transpose(ps[:, 6, 0:P], self.on[:].rearrange("p a x -> p (a x)"), K.ident[:, :])\
            .then_inc(s.sem, s.step("pe.S.turn_o"))
        pe.wait_ge(plan.dve_done, plan.value("dve.S.pT"))
        for q in range(NSEQ):
            n = NSEQ + q
            pe.wait_ge(K.sem(f"cache_loaded{n % 2}"), self.arrived(n))
            for t in range(DSEQ):
                col = 16 * q + 4 * t
                for hp in range(2):
                    for g in range(3):
                        row = self.CACHE[g] + (t if g else 0)
                        last = pe.matmul(ps[:, 5, col + 2 * hp:col + 2 * hp + 2],
                                         self.cache[:, n % 2, row, hp * P:(hp + 1) * P],
                                         self.pT[:, g, col + 2 * hp:col + 2 * hp + 2], start=(g == 0), stop=(g == 2))
            last.then_inc(s.sem, s.step(f"pe.S.o{q}"))

class MixB:

    PAIRS = 6
    KAPPA = float(np.exp(-0.5))
    LN_EPS = 64e-5

    def __init__(self, K, w0):
        self.K, self.w0 = K, w0
        a = ARENA

        def take(name, shape, dtype=F32):
            nonlocal a
            t = K.at(f"b_{name}", shape, dtype, a)
            size = 2 if dtype is BF16 else 4
            for n in shape[1:]:
                size *= n
            a += size
            return t

        RAW = 1 + SEQ + NSEQ * (DSEQ + 1)
        self.RAW = RAW
        self.raw = [take(f"raw{n}", [P, RAW]) for n in range(3)]
        self.raw_at = [ARENA + n * RAW * 4 for n in range(3)]
        self.rkv = [take(f"x{n}", [P, T]) for n in range(3)]
        self.x1_at = a - 2 * WIDE
        e_at = a
        self.e = [take(f"e{n}", [P, T]) for n in range(5)]
        self.low = take("low", [P, T])
        self.low_w = take("low_w", [P, 3, P])
        self.reset = take("reset", [P, T], BF16)
        mats = lambda n: take(n, [P, 2, 4, P])
        self.L, self.X, self.Y, self.T1, self.KA, self.RB, self.RK = map(mats, ("L", "X", "Y", "T1", "KA", "RB", "RK"))
        self.tm = [take(f"tm{n}", [P, 4, P]) for n in "bkv"]
        self.Rh = take("Rh", [P, 4, P])
        self.MT = take("MT", [P, 4, 64])
        self.N0 = take("N0", [P, 4, 64])
        self.S = take("S", [P, NB + 1, 64])
        mats = lambda n: take(n, [NS, 2, NS])
        self.sL, self.sX, self.sY, self.sT1, self.sKA, self.sRB, self.sRK = map(
            mats, ("sL", "sX", "sY", "sT1", "sKA", "sRB", "sRK"))
        self.stm = [take(f"stm{n}", [NS, P]) for n in "bkv"]
        self.sA = take("sA", [NS, 2, P])
        self.sGW = take("sGW", [NS, 2, P])
        self.sRh = take("sRh", [P, NS])
        self.sGT = take("sGT", [P, NS])
        self.sS = take("sS", [P, NSEQ, 64])
        self.mid = take("mid", [P, NB + 1])
        self.scale = take("scale", [P, NB])
        self.last = take("last", [P, 2 * (1 + NSEQ) * 0 + 16])
        assert a <= 229368, a - 229368
        self.A = K.at("b_A", [P, 2, 4, P], F32, e_at + 3 * WIDE)
        self.GW = K.at("b_GW", [P, 2, 4, P], F32, e_at + 4 * WIDE)
        self.U_s = K.at("b_U_s", [NS, NSEQ, 64], F32, self.x1_at)
        self.V_s = K.at("b_V_s", [NS, NSEQ, 64], F32, self.x1_at + NSEQ * 64 * 4)
        self.y = K.at("b_y", [P, T], F32, self.raw_at[2])
        self.g_hi = self.e[3]
        self.g_lo = self.e[4]
        act, dve = (lambda n: f"act.B.{n}"), (lambda n: f"dve.B.{n}")
        uses = [act(f"w{c}") for c in range(NT)] + [act(f"a{c}") for c in range(NT)] + [act(f"g{c}") for c in range(NT)]
        uses += [dve(f"ss{c}") for c in range(NT)] + [dve(f"bo{c}") for c in range(NT)]
        for G in "01s":
            uses += [act(f"t{x}{G}") for x in "abkv"]
            uses += [dve(f"{x}{G}{e}") for x in ("L", "N", "KA", "RB", "RK") for e in range(2)]
            uses += [act(f"LV{G}{e}") for e in range(2)]
            for m in self.levels(G):
                uses += [act(f"T{m}_{G}{e}") for e in range(2)] + [dve(f"Y{m}_{G}{e}") for e in range(2)]
                if m != self.levels(G)[-1]:
                    uses += [dve(f"X{m}_{G}{e}") for e in range(2)]
            uses += [act(f"GW{G}{e}") for e in range(2)]
            if G == "s":
                uses += [act("GTs"), dve("Rhs"), dve("Us0"), dve("Us1"), dve("SSs"), act("ys")]
            else:
                uses += [dve(f"MT{G}"), dve(f"NV{G}"), dve(f"Rh{G}")]
                uses += [dve(f"S{int(G) * 4 + c}") for c in range(4)]
                uses += [act(f"y{G}")]
        uses += [dve(f"mean{c}") for c in range(NT)] + [act(f"var{c}") for c in range(NT)]
        self.banks = Banks(K.plan, uses, 3, 5)

    def levels(self, G):
        return [m for m in LEVELS[1:] if G != "s" or m < DSEQ]

    def pe(self, pe):
        K, plan, ps = self.K, self.K.plan, self.K.psum
        s = plan.steps["pe"]
        B = self.banks
        pe.wait_ge(plan.act_done, plan.value("act.low.end"))
        with s.loop(pe, self.PAIRS) as i:
            for n in range(3):
                K.weight_ready(pe, i * 3 + (self.w0 + n))
                for c in range(NT):
                    pe.wait_ge(plan.act_done, plan.value(f"act.B.in{(n - 1) % 3}.{c}", i, 1 if n == 0 else 0))
                    plan.alone(pe, i)
                    K.product(pe, n, c, c).then_inc(s.sem, s.step(f"pe.B.in{n}.{c}"))
            w, a, g0, g1 = (self.low_w[0:64, 0], self.low_w[64:P, 0], self.low_w[:, 1], self.low_w[0:32, 2])
            pe.wait_ge(K.sem("b_low_loaded"), (i + 1) * 48)
            for name, parts in (("w", ((w, self.low[0:64]),)), ("a", ((a, self.low[64:P]),)),
                                ("g", ((g0, self.g_hi[:]), (g1, self.g_lo[0:32])))):
                for c in range(NT):
                    pe.wait_ge(*B.emptied(f"{name}{c}", i))
                    plan.alone(pe, i)
                    cols = slice(c * TC, (c + 1) * TC)
                    for n, (wt, h) in enumerate(parts):
                        last = pe.matmul(ps[:, B.of(f"{name}{c}"), 0:TC], wt, h[:, cols], start=(n == 0),
                                         stop=(n == len(parts) - 1))
                    last.then_inc(s.sem, s.step(f"pe.B.{name}{c}"))

            def sums(name, src, after):
                for c in range(NT):
                    pe.wait_ge(*B.emptied(f"{name}{c}", i))
                    plan.alone(pe, i)
                    pe.wait_ge(plan.sem(after.format(c=c)), plan.value(after.format(c=c), i))
                    plan.alone(pe, i)
                    pe.matmul(ps[:, B.of(f"{name}{c}"), 0:TC], K.half_ones[:, :], src[:, c * TC:(c + 1) * TC],
                              start=True, stop=True).then_inc(s.sem, s.step(f"pe.B.{name}{c}"))

            sums("ss", self.e[4], "act.B.kk2")
            sums("bo", self.raw[1], "dve.B.rk")
            for G in "01s":
                self.pe_group(pe, G, i)
            sums("mean", self.y, "act.B.ys")
            sums("var", self.e[3], "act.B.sq")

    def pe_group(self, pe, G, i):
        K, plan, ps = self.K, self.K.plan, self.K.psum
        s = plan.steps["pe"]
        B = self.banks
        sample = G == "s"
        tiles = [(0, slice(SEQ, T), NS)] if sample else [(j, slice((4 * int(G) + j) * P, (4 * int(G) + j + 1) * P), P)
                                                      for j in range(4)]
        R = NS if sample else P
        aT, bT, kT, rT, vT = self.e[0], self.raw[0], self.e[1], self.rkv[0], self.rkv[2]
        for x, src, after in (("a", aT, "dve.B.aT"), ("b", bT, "dve.B.bT"), ("k", kT, "dve.B.kT"), ("v", vT, "dve.B.x2s")):
            pe.wait_ge(*B.emptied(f"t{x}{G}", i))
            plan.alone(pe, i)
            pe.wait_ge(plan.sem(after), plan.value(after, i))
            plan.alone(pe, i)
            for j, cols, n in tiles:
                last = pe.transpose(ps[0:R, B.of(f"t{x}{G}"), j * P:j * P + P], src[:, cols], K.ident[:, :])
            last.then_inc(s.sem, s.step(f"pe.B.t{x}{G}"))

        def score(name, lhs, rhs, after=()):
            for e in range(2):
                pe.wait_ge(*B.emptied(f"{name}{G}{e}", i))
                plan.alone(pe, i)
                for l in after:
                    pe.wait_ge(plan.sem(l), plan.value(l, i))
                    plan.alone(pe, i)
                h = slice(64 * e, 64 * e + 64)
                for j, cols, n in tiles:
                    last = pe.matmul(ps[0:R, B.of(f"{name}{G}{e}"), j * n:j * n + n], lhs[h, cols], rhs[h, cols],
                                     start=True, stop=True)
                last.then_inc(s.sem, s.step(f"pe.B.{name}{G}{e}"))

        score("L", aT, bT)
        score("N", bT, aT)
        score("KA", kT, aT)
        score("RB", bT, rT, ["dve.B.rT"])
        score("RK", kT, rT)
        L, X, Y, T1, KA, RB, RK = ((self.sL, self.sX, self.sY, self.sT1, self.sKA, self.sRB, self.sRK) if sample
                                   else (self.L, self.X, self.Y, self.T1, self.KA, self.RB, self.RK))
        at = (lambda m, e, j: m[:, e]) if sample else (lambda m, e, j: m[:, e, j])
        tm = self.stm if sample else self.tm
        row = (lambda t, j, e: t[:, 64 * e:64 * e + 64]) if sample else (lambda t, j, e: t[:, j, 64 * e:64 * e + 64])
        A = self.sA if sample else self.A
        GW = self.sGW if sample else self.GW
        for e in range(2):
            pe.wait_ge(*B.emptied(f"LV{G}{e}", i))
            plan.alone(pe, i)
            pe.wait_ge(plan.dve_done, plan.value(f"dve.B.KA{G}{e}", i))
            plan.alone(pe, i)
            pe.wait_ge(plan.act_done, plan.value(f"act.B.tv{G}", i))
            plan.alone(pe, i)
            for j, cols, n in tiles:
                last = pe.matmul(ps[0:R, B.of(f"LV{G}{e}"), j * 64:j * 64 + 64], at(KA, e, j), row(tm[2], j, e),
                                 start=True, stop=True)
            last.then_inc(s.sem, s.step(f"pe.B.LV{G}{e}"))

        def full(name, lhs, rhs, after):
            for e in range(2):
                pe.wait_ge(*B.emptied(f"{name}_{G}{e}", i))
                plan.alone(pe, i)
                for l in after:
                    pe.wait_ge(plan.sem(f"{l}{G}{e}"), plan.value(f"{l}{G}{e}", i))
                    plan.alone(pe, i)
                for j, cols, n in tiles:
                    last = pe.matmul(ps[0:R, B.of(f"{name}_{G}{e}"), j * n:j * n + n], at(lhs, e, j), at(rhs, e, j),
                                     start=True, stop=True)
                last.then_inc(s.sem, s.step(f"pe.B.{name}_{G}{e}"))

        levels = self.levels(G)
        for m in levels:
            full(f"T{m}", L, Y, [f"dve.B.Y{m // 2}_"] if m > 2 else ["dve.B.N"])
            full(f"Y{m}", X, T1, [f"act.B.T{m}_"] + ([f"dve.B.X{m // 2}_"] if m > 2 else ["dve.B.L"]))
            if m != levels[-1]:
                full(f"X{m}", T1, X, [])
        for e in range(2):
            pe.wait_ge(*B.emptied(f"GW{G}{e}", i))
            plan.alone(pe, i)
            pe.wait_ge(plan.dve_done, plan.value(f"dve.B.Y{levels[-1]}_{G}{e}", i))
            plan.alone(pe, i)
            pe.wait_ge(plan.act_done, plan.value(f"act.B.LV{G}{e}", i))
            plan.alone(pe, i)
            for j, cols, n in tiles:
                last = pe.matmul(ps[0:R, B.of(f"GW{G}{e}"), j * P:j * P + P], at(Y, e, j), at(A, e, j),
                                 start=True, stop=True)
            last.then_inc(s.sem, s.step(f"pe.B.GW{G}{e}"))
        gw = (lambda e, j, w: GW[:, e, 64 * w:64 * w + 64]) if sample else (lambda e, j, w: GW[:, e, j, 64 * w:64 * w + 64])
        if sample:
            pe.wait_ge(*B.emptied("GTs", i))
            plan.alone(pe, i)
            for e in range(2):
                last = pe.matmul(ps[64 * e:64 * e + 64, B.of("GTs"), 0:NS], A[:, e, 0:64], Y[:, e],
                                 start=True, stop=True)
            last.then_inc(s.sem, s.step("pe.B.GTs"))
        else:
            for name in ("MT", "NV"):
                pe.wait_ge(*B.emptied(f"{name}{G}", i))
                plan.alone(pe, i)
                for e in range(2):
                    pe.wait_ge(plan.act_done, plan.value(f"act.B.GW{G}{e}", i))
                    plan.alone(pe, i)
                    for j, cols, n in tiles:
                        out = ps[64 * e:64 * e + 64, B.of(f"{name}{G}"), j * 64:j * 64 + 64]
                        if name == "MT":
                            last = pe.matmul(out, gw(e, j, 0), row(tm[0], j, e), start=True, stop=True)
                        else:
                            pe.matmul(out, row(tm[0], j, e), gw(e, j, 1), start=True, stop=False)
                            last = pe.matmul(out, row(tm[1], j, e), row(tm[2], j, e), start=False, stop=True)
                last.then_inc(s.sem, s.step(f"pe.B.{name}{G}"))
        pe.wait_ge(*B.emptied(f"Rh{G}", i))
        plan.alone(pe, i)
        for e in range(2):
            pe.wait_ge(plan.dve_done, plan.value(f"dve.B.RB{G}{e}", i))
            plan.alone(pe, i)
            pe.wait_ge(plan.act_done, plan.value(f"act.B.GW{G}{e}", i))
            plan.alone(pe, i)
            for j, cols, n in tiles:
                last = pe.matmul(ps[64 * e:64 * e + 64, B.of(f"Rh{G}"), j * n:j * n + n], gw(e, j, 0), at(RB, e, j),
                                 start=True, stop=True)
        last.then_inc(s.sem, s.step(f"pe.B.Rh{G}"))
        if sample:
            pe.wait_ge(K.sem("b_state_loaded"), (i + 1) * 16)
            pe.wait_ge(plan.act_done, plan.value("act.B.GTs", i))
            plan.alone(pe, i)
            for e in range(2):
                pe.wait_ge(*B.emptied(f"Us{e}", i))
                plan.alone(pe, i)
                h = slice(64 * e, 64 * e + 64)
                pe.matmul(ps[0:NS, B.of(f"Us{e}"), :], self.sGT[h, :], flat(self.sS[h]), start=True, stop=True)\
                    .then_inc(s.sem, s.step(f"pe.B.Us{e}"))
            pe.wait_ge(*B.emptied("SSs", i))
            plan.alone(pe, i)
            for e in range(2):
                h = slice(64 * e, 64 * e + 64)
                pe.wait_ge(plan.dve_done, plan.value(f"dve.B.Ux{e}", i))
                plan.alone(pe, i)
                pe.matmul(ps[h, B.of("SSs"), :], row(tm[0], 0, e), flat(self.U_s[:]), start=True, stop=False)
                pe.matmul(ps[h, B.of("SSs"), :], row(tm[1], 0, e), flat(self.V_s[:]), start=False, stop=True)\
                    .then_inc(s.sem, s.step(f"pe.B.SS{e}"))
        else:
            for c in range(4):
                b = 4 * int(G) + c
                pe.wait_ge(*B.emptied(f"S{b}", i))
                plan.alone(pe, i)
                if b:
                    pe.wait_ge(plan.dve_done, plan.value(f"dve.B.S{b - 1}", i))
                    plan.alone(pe, i)
                pe.wait_ge(plan.dve_done, plan.value(f"dve.B.NV{G}", i))
                plan.alone(pe, i)
                for e in range(2):
                    h = slice(64 * e, 64 * e + 64)
                    last = pe.matmul(ps[h, B.of(f"S{b}"), 0:64], self.MT[h, c], self.S[h, b], start=True, stop=True)
                last.then_inc(s.sem, s.step(f"pe.B.S{b}"))
        pe.wait_ge(*B.emptied(f"y{G}", i))
        plan.alone(pe, i)
        pe.wait_ge(plan.dve_done, plan.value(f"dve.B.Rh{G}", i))
        plan.alone(pe, i)
        for e in range(2):
            pe.wait_ge(plan.dve_done, plan.value(f"dve.B.RK{G}{e}", i))
            plan.alone(pe, i)
            h = slice(64 * e, 64 * e + 64)
            for j, cols, n in tiles:
                out = ps[h, B.of(f"y{G}"), j * n:j * n + n]
                pe.matmul(out, gw(e, j, 1), at(RB, e, j), start=True, stop=False)
                last = pe.matmul(out, row(tm[2], j, e), at(RK, e, j), start=False, stop=sample)
                if not sample:
                    last = pe.matmul(out, self.S[h, 4 * int(G) + j], self.Rh[h, j], start=False, stop=True)
            if sample:
                for q in range(NSEQ):
                    c = slice(DSEQ * q, DSEQ * q + DSEQ)
                    last = pe.matmul(ps[h, B.of("ys"), c], self.sS[h, q], self.sRh[h, c], start=False, stop=True,
                                     skip_group_check=True)
        last.then_inc(s.sem, s.step(f"pe.B.y{G}"))

    def act(self, act):
        K, plan, ps = self.K, self.K.plan, self.K.psum
        s = plan.steps["act"]
        B = self.banks
        for name in ("b_prompt_state_stored", "b_state_stored", "b_out_stored"):
            act.sem_inc(K.sem(name), 16)
        with s.loop(act, self.PAIRS) as i:
            act.wait_ge(plan.pe_done, plan.value("pe.B.ys", i, 1))
            plan.alone(act, i)
            act.wait_ge(plan.pe_done, plan.value("pe.B.var2", i, 1))
            plan.alone(act, i)
            act.wait_ge(plan.dve_done, plan.value("dve.B.out", i, 1))
            plan.alone(act, i)
            act.wait_ge(K.sem("b_state_stored"), (i + 1) * 16)
            loaded = K.sem("b_low_loaded")
            act.dma_start(flat(self.low_w[:]), K.io["low_w"][bass.ds(i, 1)].rearrange("o p n -> (o p) n")).then_inc(loaded, 16)
            act.dma_start(self.g_hi[:], K.io["b_gd"][0]).then_inc(loaded, 16)
            act.dma_start(self.g_lo[0:32], K.io["b_gd"][1, 0:32]).then_inc(loaded, 16)
            act.dma_start(flat(self.sS[:]), K.io["state_b"][bass.ds(i, 1)].rearrange("o p n -> (o p) n"))\
                .then_inc(K.sem("b_state_loaded"), 16)
            for n in range(3):
                for c in range(NT):
                    act.wait_ge(plan.pe_done, plan.value(f"pe.B.in{n}.{c}", i))
                    plan.alone(act, i)
                    src = ps[:, c, 0:TC]
                    if c < NT - 1:
                        act.activation(self.raw[n][:, 1 + c * TC:1 + (c + 1) * TC], src, ACT.Copy)\
                            .then_inc(s.sem, s.step(f"act.B.in{n}.{c}"))
                    else:
                        w = SEQ - c * TC
                        act.activation(self.raw[n][:, 1 + c * TC:1 + SEQ], src[:, 0:w], ACT.Copy)\
                            .then_inc(s.sem, s.step())
                        seqs = self.raw[n][:, 1 + SEQ:].rearrange("p (q w) -> p q w", w=DSEQ + 1)[:, :, 1:]
                        act.activation(seqs, src[:, w:TC].rearrange("p (q w) -> p q w", w=DSEQ), ACT.Copy)\
                            .then_inc(s.sem, s.step(f"act.B.in{n}.{c}"))
            col = lambda name: K.vec[:, bass.ds(i + VEC[name][0], 1)]
            for name, dst, func, bias in (("w", 0, ACT.Sigmoid, "w0"), ("a", 1, ACT.Sigmoid, "a0"), ("g", 2, ACT.Copy, None)):
                for c in range(NT):
                    act.wait_ge(plan.pe_done, plan.value(f"pe.B.{name}{c}", i))
                    plan.alone(act, i)
                    kw = dict(bias=col(bias)) if bias else {}
                    act.activation(self.e[dst][:, c * TC:(c + 1) * TC], ps[:, B.of(f"{name}{c}"), 0:TC], func, **kw)\
                        .then_inc(s.sem, s.step(f"act.B.{name}{c}"))
            act.wait_ge(plan.dve_done, plan.value("dve.B.x1s", i))
            plan.alone(act, i)
            act.wait_ge(plan.pe_done, plan.value("pe.B.g2", i))
            plan.alone(act, i)
            act.activation(self.e[4][:], self.rkv[1][:], ACT.Square, scale=col("k_k"))\
                .then_inc(s.sem, s.step("act.B.kk2"))
            act.wait_ge(plan.dve_done, plan.value("dve.B.ss2", i))
            plan.alone(act, i)
            act.activation(self.raw[0][:, 0:T], self.raw[0][:, 0:T], ACT.Sqrt).then_inc(s.sem, s.step("act.B.norm"))
            act.wait_ge(plan.dve_done, plan.value("dve.B.cx", i))
            plan.alone(act, i)
            act.activation(self.e[0][:], self.e[0][:], ACT.Exp, scale=-self.KAPPA)\
                .then_inc(s.sem, s.step("act.B.pex"))
            act.wait_ge(plan.pe_done, plan.value("pe.B.ss2", i))
            plan.alone(act, i)
            act.activation(self.e[4][:], self.e[3][:], ACT.Exp, scale=-self.KAPPA)\
                .then_inc(s.sem, s.step("act.B.pin"))
            act.wait_ge(plan.act_done, plan.value("act.B.pin", i))
            plan.alone(act, i)
            act.activation(self.e[3][:], self.e[3][:], ACT.Exp, scale=self.KAPPA)\
                .then_inc(s.sem, s.step("act.B.pinv"))
            act.wait_ge(plan.dve_done, plan.value("dve.B.mid_sum", i))
            plan.alone(act, i)
            act.activation(self.scale[:], self.scale[:], ACT.Exp, scale=-self.KAPPA)\
                .then_inc(s.sem, s.step("act.B.scale"))
            for G in "01s":
                self.act_group(act, G, i)
            act.wait_ge(plan.dve_done, plan.value("dve.B.mean2", i))
            plan.alone(act, i)
            act.activation(self.e[3][:], self.y[:], ACT.Square).then_inc(s.sem, s.step("act.B.sq"))
            for c in range(NT):
                act.wait_ge(plan.pe_done, plan.value(f"pe.B.var{c}", i))
                plan.alone(act, i)
                act.activation(self.e[4][:, c * TC:(c + 1) * TC], ps[:, B.of(f"var{c}"), 0:TC], ACT.Sqrt,
                               scale=1.0 / 64, bias=K.derived[:, 3:4]).then_inc(s.sem, s.step(f"act.B.var{c}"))
            act.wait_ge(plan.dve_done, plan.value("dve.B.out", i))
            plan.alone(act, i)
            act.dma_start(K.io["mix"][bass.ds(i + 2, 1)].rearrange("o p t -> (o p) t"), self.y[:])\
                .then_inc(K.sem("b_out_stored"), 16)
            act.wait_ge(plan.dve_done, plan.value("dve.B.S7", i))
            plan.alone(act, i)
            act.dma_start(K.io["p_wkv"][bass.ds(i, 1)].rearrange("o p n -> (o p) n"), self.S[:, NB])\
                .then_inc(K.sem("b_prompt_state_stored"), 16)
            act.wait_ge(plan.dve_done, plan.value("dve.B.sS", i))
            plan.alone(act, i)
            act.dma_start(K.io["s_wkv"][bass.ds(i, 1)].rearrange("o p n -> (o p) n"), flat(self.sS[:]))\
                .then_inc(K.sem("b_state_stored"), 16)
            act.wait_ge(K.sem("b_out_stored"), (i + 2) * 16)
        for name in ("b_prompt_state_stored", "b_state_stored", "b_out_stored"):
            act.wait_ge(K.sem(name), (self.PAIRS + 1) * 16)

    def act_group(self, act, G, i):
        K, plan, ps = self.K, self.K.plan, self.K.psum
        s = plan.steps["act"]
        B = self.banks
        sample = G == "s"
        R = NS if sample else P
        prev = {"0": ("1", 1), "1": ("0", 0)}
        if not sample:
            g, lag = prev[G]
            act.wait_ge(plan.pe_done, plan.value(f"pe.B.y{g}", i, lag))
            plan.alone(act, i)
        n = NS if sample else P
        src = ps[0:R, B.of(f"ta{G}"), 0:P if sample else 512]
        act.wait_ge(plan.pe_done, plan.value(f"pe.B.ta{G}", i))
        plan.alone(act, i)
        if sample:
            act.activation(self.sA[:, :, 0:64], src.rearrange("p (e x) -> p e x", e=2), ACT.Copy)\
                .then_inc(s.sem, s.step(f"act.B.ta{G}"))
        else:
            if G == "0":
                act.wait_ge(plan.dve_done, plan.value("dve.B.bT", i))
                plan.alone(act, i)
                act.wait_ge(plan.dve_done, plan.value("dve.B.kT", i))
                plan.alone(act, i)
            act.activation(self.A[:, :, :, 0:64].rearrange("p e j x -> p j e x"),
                           src.rearrange("p (j e x) -> p j e x", j=4, e=2), ACT.Copy)\
                .then_inc(s.sem, s.step(f"act.B.ta{G}"))
        for x, dst in zip("bkv", self.stm if sample else self.tm):
            act.wait_ge(plan.pe_done, plan.value(f"pe.B.t{x}{G}", i))
            plan.alone(act, i)
            act.activation(dst[:] if sample else flat(dst[:]),
                           ps[0:R, B.of(f"t{x}{G}"), 0:P if sample else 512], ACT.Copy)\
                .then_inc(s.sem, s.step(f"act.B.t{x}{G}"))
        A = self.sA if sample else self.A
        for e in range(2):
            act.wait_ge(plan.pe_done, plan.value(f"pe.B.LV{G}{e}", i))
            plan.alone(act, i)
            if sample:
                act.activation(A[:, e, 64:P], ps[0:R, B.of(f"LV{G}{e}"), 0:64], ACT.Copy)\
                    .then_inc(s.sem, s.step(f"act.B.LV{G}{e}"))
            else:
                act.activation(A[:, e, :, 64:P], ps[:, B.of(f"LV{G}{e}"), 0:256].rearrange("p (j x) -> p j x", j=4),
                               ACT.Copy).then_inc(s.sem, s.step(f"act.B.LV{G}{e}"))
        T1 = self.sT1 if sample else self.T1
        for m in self.levels(G):
            for e in range(2):
                act.wait_ge(plan.pe_done, plan.value(f"pe.B.T{m}_{G}{e}", i))
                plan.alone(act, i)
                if m > 2:
                    act.wait_ge(plan.pe_done, plan.value(f"pe.B.X{m // 2}_{G}{e}", i))
                    plan.alone(act, i)
                dst = T1[:, e] if sample else flat(T1[:, e])
                act.activation(dst, ps[0:R, B.of(f"T{m}_{G}{e}"), 0:NS if sample else 512], ACT.Copy)\
                    .then_inc(s.sem, s.step(f"act.B.T{m}_{G}{e}"))
        GW = self.sGW if sample else self.GW
        for e in range(2):
            act.wait_ge(plan.pe_done, plan.value(f"pe.B.GW{G}{e}", i))
            plan.alone(act, i)
            if G == "0" and e == 0:
                act.wait_ge(plan.dve_done, plan.value("dve.B.rT", i))
                plan.alone(act, i)
                act.wait_ge(plan.dve_done, plan.value("dve.B.sEnd", i))
                plan.alone(act, i)
            dst = GW[:, e] if sample else flat(GW[:, e])
            act.activation(dst, ps[0:R, B.of(f"GW{G}{e}"), 0:P if sample else 512], ACT.Copy)\
                .then_inc(s.sem, s.step(f"act.B.GW{G}{e}"))
        if sample:
            act.wait_ge(plan.pe_done, plan.value("pe.B.GTs", i))
            plan.alone(act, i)
            act.activation(self.sGT[:], ps[:, B.of("GTs"), 0:NS], ACT.Copy).then_inc(s.sem, s.step("act.B.GTs"))
        act.wait_ge(plan.pe_done, plan.value(f"pe.B.y{G}", i))
        plan.alone(act, i)
        if G == "0":
            act.wait_ge(plan.dve_done, plan.value("dve.B.x2s", i))
            plan.alone(act, i)
        cols = slice(SEQ, T) if sample else slice(4 * int(G) * P, 4 * (int(G) + 1) * P)
        act.activation(self.y[:, cols], ps[:, B.of(f"y{G}"), 0:NS if sample else 512], ACT.Copy)\
            .then_inc(s.sem, s.step(f"act.B.y{G}"))

    def dve(self, dve):
        K, plan, ps = self.K, self.K.plan, self.K.psum
        s = plan.steps["dve"]
        B = self.banks
        for t in (self.L, self.KA, self.RB, self.RK, self.sL, self.sKA, self.sRB, self.sRK):
            dve.memset(t[:], 0.0).then_inc(s.sem, s.step())
        dve.memset(self.S[:, 0], 0.0).then_inc(s.sem, s.step())
        dve.memset(K.derived[:, 3:4], self.LN_EPS).then_inc(s.sem, s.step("dve.B.zero"))
        dve.wait_ge(plan.dve_done, plan.value("dve.B.zero"))
        col = lambda name: K.vec[:, bass.ds(i + VEC[name][0], 1)]
        e0, e1, e2, e3, e4 = (t[:] for t in self.e)
        with s.loop(dve, self.PAIRS) as i:
            def op(instruction, name):
                instruction.then_inc(s.sem, s.step(f"dve.B.{name}"))
                dve.wait_ge(plan.dve_done, plan.value(f"dve.B.{name}", i))
                plan.alone(dve, i)
            for n in range(3):
                raw, x = self.raw[n], self.rkv[n]
                dve.wait_ge(plan.act_done, plan.value(f"act.B.in{n}.{NT - 1}", i))
                plan.alone(dve, i)
                if n == 0:
                    dve.wait_ge(plan.pe_done, plan.value("pe.B.ys", i, 1))
                    plan.alone(dve, i)
                    dve.wait_ge(plan.dve_done, plan.value("dve.B.out", i, 1))
                    plan.alone(dve, i)
                mid = raw[:, 1 + SEQ:].rearrange("p (q w) -> p q w", w=DSEQ + 1)
                dve.memset(raw[:, 0:1], 0.0).then_inc(s.sem, s.step())
                op(dve.tensor_copy(mid[:, :, 0], K.shift[:, bass.ds(i * 8 + 48 * n, 8)]), f"z{n}")
                mu = K.vec[:, bass.ds(i + (VEC["mu"][0] + 6 * n), 1)]
                xs = x[:, SEQ:T].rearrange("p (q w) -> p q w", w=DSEQ)
                last = K.last_rows
                dve.tensor_copy(last[:, bass.ds(i * 9 + 54 * n, 1)], raw[:, SEQ:SEQ + 1]).then_inc(s.sem, s.step())
                dve.tensor_copy(last[:, bass.ds(i * 9 + (54 * n + 1), 8)], mid[:, :, DSEQ]).then_inc(s.sem, s.step())
                dve.tensor_tensor(x[:, 0:SEQ], raw[:, 0:SEQ], raw[:, 1:1 + SEQ], ALU.subtract)\
                    .then_inc(s.sem, s.step())
                op(dve.tensor_tensor(xs, mid[:, :, 0:DSEQ], mid[:, :, 1:], ALU.subtract), f"d{n}")
                dve.scalar_tensor_tensor(out=x[:, 0:SEQ], in0=x[:, 0:SEQ], scalar=mu, in1=raw[:, 1:1 + SEQ],
                                         op0=ALU.mult, op1=ALU.add).then_inc(s.sem, s.step())
                op(dve.scalar_tensor_tensor(out=xs, in0=xs, scalar=mu, in1=mid[:, :, 1:], op0=ALU.mult, op1=ALU.add),
                   f"x{n}s")
            dve.wait_ge(plan.act_done, plan.value("act.B.w2", i))
            plan.alone(dve, i)
            dve.wait_ge(plan.pe_done, plan.value("pe.B.g2", i))
            plan.alone(dve, i)
            op(dve.tensor_tensor_scan(out=e3, data0=self.reset[:], data1=e0, initial=0.0, op0=ALU.mult, op1=ALU.add), "c")
            tiles = self.e[3][:, 0:SEQ].rearrange("p (b t) -> p b t", t=P)
            dve.memset(self.mid[:, NB:NB + 1], 0.0).then_inc(s.sem, s.step())
            op(dve.tensor_copy(self.mid[:, 0:NB], tiles[:, :, P // 2 - 1]), "mid")
            op(dve.tensor_tensor(tiles, tiles, self.mid[:, 0:NB].unsqueeze(2).broadcast_to([P, NB, P]), ALU.subtract), "cm")
            op(dve.tensor_tensor(self.scale[:], tiles[:, :, P - 1], self.mid[:, 1:NB + 1], ALU.add), "mid_sum")
            op(dve.tensor_tensor(e0, e3, e0, ALU.subtract), "cx")
            for c in range(NT):
                dve.wait_ge(plan.pe_done, plan.value(f"pe.B.ss{c}", i))
                plan.alone(dve, i)
                dve.tensor_scalar(self.raw[0][:, c * TC:(c + 1) * TC], ps[:, B.of(f"ss{c}"), 0:TC], 1e-24, None,
                                  ALU.max).then_inc(s.sem, s.step(f"dve.B.ss{c}"))
            r0, r1 = self.raw[0][:, 0:T], self.raw[1][:, 0:T]
            r, k, v = (t[:] for t in self.rkv)
            dve.wait_ge(plan.act_done, plan.value("act.B.norm", i))
            plan.alone(dve, i)
            op(dve.reciprocal(r0, r0), "inv")
            op(dve.scalar_tensor_tensor(out=r0, in0=k, scalar=col("k_k"), in1=r0, op0=ALU.mult, op1=ALU.mult), "kk")
            dve.wait_ge(plan.act_done, plan.value("act.B.a2", i))
            plan.alone(dve, i)
            dve.tensor_scalar(r1, e1, col("k_a"), K.one_less_ka[:, bass.ds(i, 1)], ALU.mult, ALU.add)\
                .then_inc(s.sem, s.step())
            dve.wait_ge(plan.act_done, plan.value("act.B.pex", i))
            plan.alone(dve, i)
            dve.scalar_tensor_tensor(out=e0, in0=r0, scalar=-1.0, in1=e0, op0=ALU.mult, op1=ALU.mult)\
                .then_inc(s.sem, s.step("dve.B.aT"))
            op(dve.tensor_tensor(r0, r0, e1, ALU.mult), "kka")
            dve.wait_ge(plan.act_done, plan.value("act.B.pinv", i))
            plan.alone(dve, i)
            dve.tensor_tensor(r0, r0, e3, ALU.mult).then_inc(s.sem, s.step("dve.B.bT"))
            op(dve.tensor_tensor(e1, k, r1, ALU.mult), "kmod")
            op(dve.scalar_tensor_tensor(out=r1, in0=r, scalar=col("r_k"), in1=e1, op0=ALU.mult, op1=ALU.mult), "rk")
            dve.tensor_tensor(e1, e1, e3, ALU.mult).then_inc(s.sem, s.step("dve.B.kT"))
            dve.tensor_tensor(r, r, e4, ALU.mult).then_inc(s.sem, s.step("dve.B.rT"))
            op(dve.tensor_copy(self.last[:, 0:8], self.e[4][:, SEQ:T].rearrange("p (q w) -> p q w", w=DSEQ)[:, :, DSEQ - 1]),
               "sEnd")
            for c in range(NT):
                dve.wait_ge(plan.pe_done, plan.value(f"pe.B.bo{c}", i))
                plan.alone(dve, i)
                if c == 0:
                    dve.wait_ge(plan.pe_done, plan.value("pe.B.bo2", i))
                    plan.alone(dve, i)
                cols = slice(c * TC, (c + 1) * TC)
                dve.tensor_tensor(self.raw[1][:, cols], ps[:, B.of(f"bo{c}"), 0:TC], self.rkv[2][:, cols], ALU.mult)\
                    .then_inc(s.sem, s.step(f"dve.B.bo{c}"))
            for G in "01s":
                self.dve_group(dve, G, i)
            dve.wait_ge(plan.act_done, plan.value("act.B.ys", i))
            plan.alone(dve, i)
            y = self.y[:]
            dve.wait_ge(plan.pe_done, plan.value("pe.B.mean2", i))
            plan.alone(dve, i)
            for c in range(NT):
                cols = slice(c * TC, (c + 1) * TC)
                dve.scalar_tensor_tensor(out=self.y[:, cols], in0=ps[:, B.of(f"mean{c}"), 0:TC], scalar=-1.0 / 64,
                                         in1=self.y[:, cols], op0=ALU.mult, op1=ALU.add)\
                    .then_inc(s.sem, s.step(f"dve.B.mean{c}"))
            dve.wait_ge(plan.act_done, plan.value("act.B.var2", i))
            plan.alone(dve, i)
            op(dve.reciprocal(e4, e4), "rstd")
            op(dve.scalar_tensor_tensor(out=y, in0=y, scalar=col("lnx_w"), in1=e4, op0=ALU.mult, op1=ALU.mult), "ln")
            op(dve.scalar_tensor_tensor(out=y, in0=y, scalar=col("lnx_b"), in1=r1, op0=ALU.add, op1=ALU.add), "lnb")
            dve.tensor_tensor(y, y, e2, ALU.mult).then_inc(s.sem, s.step("dve.B.out"))

    def dve_group(self, dve, G, i):
        K, plan, ps = self.K, self.K.plan, self.K.psum
        s = plan.steps["dve"]
        B = self.banks
        sample = G == "s"
        R = NS if sample else P
        L, X, Y, KA, RB, RK = ((self.sL, self.sX, self.sY, self.sKA, self.sRB, self.sRK) if sample
                               else (self.L, self.X, self.Y, self.KA, self.RB, self.RK))

        def pick(dst, mask, name, label=None):
            if sample:
                ins = dve.copy_predicated(dst, K.masks[0:NS, mask, 0:NS], ps[0:NS, B.of(name), 0:NS])
            else:
                ins = dve.copy_predicated(dst, K.masks[:, mask].unsqueeze(1).broadcast_to([P, 4, P]),
                                          ps[:, B.of(name), :].rearrange("p (j t) -> p j t", j=4))
            ins.then_inc(s.sem, s.step(label or f"dve.B.{name}"))

        lower, upper, upper_eq = (20, 18, 19) if sample else (LOWER, UPPER, UPPER_EQ)
        g, lag = {"0": ("1", 1), "1": ("0", 0), "s": ("s", 1)}[G]
        dve.wait_ge(plan.pe_done, plan.value(f"pe.B.y{g}", i, lag))
        plan.alone(dve, i)
        dve.wait_ge(plan.dve_done, plan.before(f"dve.B.X0_{G}", i))
        plan.alone(dve, i)
        ident = (K.ident[0:NS, 0:NS].unsqueeze(1).broadcast_to([NS, 2, NS]) if sample else
                 K.ident[:, :].unsqueeze(1).broadcast_to([P, 8, P]))
        whole = (lambda t: t[:]) if sample else (lambda t: t[:].rearrange("p e j t -> p (e j) t"))
        dve.tensor_copy(whole(X), ident).then_inc(s.sem, s.step(f"dve.B.X0_{G}"))
        dve.tensor_copy(whole(Y), ident).then_inc(s.sem, s.step(f"dve.B.Y0_{G}"))
        dve.wait_ge(plan.dve_done, plan.value(f"dve.B.Y0_{G}", i))
        plan.alone(dve, i)
        for e in range(2):
            dve.wait_ge(plan.pe_done, plan.value(f"pe.B.L{G}{e}", i))
            plan.alone(dve, i)
            pick(X[:, e], 7, f"L{G}{e}", f"dve.B.X1_{G}{e}")
            pick(L[:, e], lower, f"L{G}{e}")
        for e in range(2):
            dve.wait_ge(plan.pe_done, plan.value(f"pe.B.N{G}{e}", i))
            plan.alone(dve, i)
            pick(Y[:, e], 0, f"N{G}{e}")
        for name, dst, mask in (("KA", KA, upper), ("RB", RB, upper_eq), ("RK", RK, upper_eq)):
            for e in range(2):
                dve.wait_ge(plan.pe_done, plan.value(f"pe.B.{name}{G}{e}", i))
                plan.alone(dve, i)
                pick(dst[:, e], mask, f"{name}{G}{e}")
        levels = self.levels(G)
        for m in levels:
            n = LEVELS.index(m)
            for e in range(2):
                dve.wait_ge(plan.pe_done, plan.value(f"pe.B.Y{m}_{G}{e}", i))
                plan.alone(dve, i)
                pick(Y[:, e], n, f"Y{m}_{G}{e}")
            if m != levels[-1]:
                for e in range(2):
                    dve.wait_ge(plan.pe_done, plan.value(f"pe.B.X{m}_{G}{e}", i))
                    plan.alone(dve, i)
                    pick(X[:, e], 7 + n, f"X{m}_{G}{e}")
        if sample:
            dve.wait_ge(plan.pe_done, plan.value("pe.B.Rhs", i))
            plan.alone(dve, i)
            dve.tensor_tensor(self.sRh[:], ps[:, B.of("Rhs"), 0:NS], self.rkv[0][:, SEQ:T], ALU.add)\
                .then_inc(s.sem, s.step("dve.B.Rhs"))
            seqs = K.seq_mask[:, :].unsqueeze(2).broadcast_to([NS, NSEQ, 64])
            for e in range(2):
                dve.wait_ge(plan.pe_done, plan.value(f"pe.B.Us{e}", i))
                plan.alone(dve, i)
                if e:
                    dve.wait_ge(plan.pe_done, plan.value("pe.B.SS0", i))
                    plan.alone(dve, i)
                w = self.sGW[:, e, 64:P].unsqueeze(1).broadcast_to([NS, NSEQ, 64])
                dve.tensor_tensor(self.U_s[:], ps[0:NS, B.of(f"Us{e}"), :].rearrange("p (q x) -> p q x", q=NSEQ),
                                  w, ALU.add).then_inc(s.sem, s.step(f"dve.B.Us{e}"))
                dve.wait_ge(plan.dve_done, plan.value(f"dve.B.Us{e}", i))
                plan.alone(dve, i)
                dve.tensor_tensor(self.U_s[:], self.U_s[:], seqs, ALU.mult).then_inc(s.sem, s.step())
                vals = self.stm[2][:, 64 * e:64 * e + 64].unsqueeze(1).broadcast_to([NS, NSEQ, 64])
                dve.tensor_tensor(self.V_s[:], vals, seqs, ALU.mult).then_inc(s.sem, s.step(f"dve.B.Ux{e}"))
            dve.wait_ge(plan.pe_done, plan.value("pe.B.ys", i))
            plan.alone(dve, i)
            dve.tensor_tensor(flat(self.sS[:]), flat(self.sS[:]), ps[:, B.of("SSs"), :], ALU.add)\
                .then_inc(s.sem, s.step("dve.B.SSs"))
            dve.wait_ge(plan.dve_done, plan.value("dve.B.SSs", i))
            plan.alone(dve, i)
            dve.tensor_tensor(self.sS[:], self.sS[:], self.last[:, 0:8].unsqueeze(2).broadcast_to([P, NSEQ, 64]),
                              ALU.mult).then_inc(s.sem, s.step("dve.B.sS"))
            return
        dve.wait_ge(plan.pe_done, plan.value(f"pe.B.MT{G}", i))
        plan.alone(dve, i)
        dve.tensor_tensor(self.MT[:], ps[:, B.of(f"MT{G}"), 0:256].rearrange("p (j x) -> p j x", j=4),
                          K.ident2[:, :].unsqueeze(1).broadcast_to([P, 4, 64]), ALU.add)\
            .then_inc(s.sem, s.step(f"dve.B.MT{G}"))
        dve.wait_ge(plan.pe_done, plan.value(f"pe.B.NV{G}", i))
        plan.alone(dve, i)
        dve.wait_ge(plan.act_done, plan.value("act.B.scale", i))
        plan.alone(dve, i)
        dve.tensor_tensor(self.N0[:], ps[:, B.of(f"NV{G}"), 0:256].rearrange("p (j x) -> p j x", j=4),
                          self.scale[:, 4 * int(G):4 * int(G) + 4].unsqueeze(2).broadcast_to([P, 4, 64]), ALU.mult)\
            .then_inc(s.sem, s.step(f"dve.B.NV{G}"))
        dve.wait_ge(plan.pe_done, plan.value(f"pe.B.Rh{G}", i))
        plan.alone(dve, i)
        dve.tensor_tensor(flat(self.Rh[:]), ps[:, B.of(f"Rh{G}"), :],
                          self.rkv[0][:, 4 * int(G) * P:4 * (int(G) + 1) * P], ALU.add)\
            .then_inc(s.sem, s.step(f"dve.B.Rh{G}"))
        if G == "1":
            dve.wait_ge(K.sem("b_prompt_state_stored"), (i + 1) * 16)
        for c in range(4):
            b = 4 * int(G) + c
            dve.wait_ge(plan.pe_done, plan.value(f"pe.B.S{b}", i))
            plan.alone(dve, i)
            dve.wait_ge(plan.dve_done, plan.before(f"dve.B.S{b}", i))
            plan.alone(dve, i)
            dve.scalar_tensor_tensor(out=self.S[:, b + 1], in0=ps[:, B.of(f"S{b}"), 0:64],
                                     scalar=self.scale[:, b:b + 1], in1=self.N0[:, c], op0=ALU.mult, op1=ALU.add)\
                .then_inc(s.sem, s.step(f"dve.B.S{b}"))

    def pool(self, pool, before):
        K = self.K
        with K.plan.steps["pool"].loop(pool, self.PAIRS) as i:
            for n in range(3):
                pool.wait_ge(K.plan.pe_done, K.plan.value(f"pe.B.in{n}.{NT - 1}", i, 1))
                K.plan.alone(pool, i)
                if before[n]:
                    pool.wait_ge(K.plan.sem(before[n]), K.plan.value(before[n]))
                K.split_weight(pool, i * 3 + (self.w0 + n), n)


class LowRank:

    def __init__(self, K, w0, mixer):
        self.K, self.w0, self.m = K, w0, mixer

    def pe(self, pe):
        K, plan = self.K, self.K.plan
        for n in range(3):
            K.weight_ready(pe, self.w0 + n)
            for c in range(NT):
                pe.wait_ge(plan.sem(f"act.low.in{n - 1}.{c}" if n else f"act.A2.in5.{c}"), plan.value(f"act.low.in{n - 1}.{c}" if n else f"act.A2.in5.{c}"))
                K.product(pe, (n + 1) % 2, c, c)\
                    .then_inc(plan.steps["pe"].sem, plan.steps["pe"].step(f"pe.low.in{n}.{c}"))

    def act(self, act):
        K, plan, ps, m = self.K, self.K.plan, self.K.psum, self.m
        s = plan.steps["act"]
        for n in range(3):
            raw = m.raw[n]
            for c in range(NT):
                act.wait_ge(plan.pe_done, plan.value(f"pe.low.in{n}.{c}"))
                src = ps[:, c, 0:TC]
                if c < NT - 1:
                    act.activation(raw[:, 1 + c * TC:1 + (c + 1) * TC], src, ACT.Copy)\
                        .then_inc(s.sem, s.step(f"act.low.in{n}.{c}"))
                else:
                    w = SEQ - c * TC
                    act.activation(raw[:, 1 + c * TC:1 + SEQ], src[:, 0:w], ACT.Copy).then_inc(s.sem, s.step())
                    seqs = raw[:, 1 + SEQ:].rearrange("p (q w) -> p q w", w=DSEQ + 1)[:, :, 1:]
                    act.activation(seqs, src[:, w:TC].rearrange("p (q w) -> p q w", w=DSEQ), ACT.Copy)\
                        .then_inc(s.sem, s.step(f"act.low.in{n}.{c}"))
        act.wait_ge(plan.dve_done, plan.value("dve.low.x2"))
        act.activation(m.low[0:64], m.low[0:64], ACT.Tanh).then_inc(s.sem, s.step("act.low.tanh"))
        for n in (1, 2):
            act.activation(m.rkv[n][:], m.rkv[n][:], ACT.Sigmoid).then_inc(s.sem, s.step(f"act.low.sig{n}"))
            act.wait_ge(plan.act_done, plan.value(f"act.low.sig{n}"))
            act.dma_start(K.io["b_gd"][n - 1], m.rkv[n][:]).then_inc(K.sem("low_stored"), 16)
        act.wait_ge(K.sem("low_stored"), 32)
        act.copy(K.derived[:, 4:5], K.derived[:, 1:2]).then_inc(s.sem, s.step("act.low.end"))

    def dve(self, dve):
        K, plan, m = self.K, self.K.plan, self.m
        s = plan.steps["dve"]
        for n in range(3):
            dve.memset(m.raw[n][:, 0:1], 0.0).then_inc(s.sem, s.step())
            pads = m.raw[n][:, 1 + SEQ:].rearrange("p (q w) -> p q w", w=DSEQ + 1)[:, :, 0]
            dve.tensor_copy(pads, K.shift[:, 8 * (18 + n):8 * (19 + n)]).then_inc(s.sem, s.step())
        dve.memset(m.reset[:], 1.0).then_inc(s.sem, s.step("dve.low.ones"))
        dve.wait_ge(plan.dve_done, plan.value("dve.low.ones"))
        dve.memset(m.reset[:, 0:SEQ].rearrange("p (b t) -> p b t", t=P)[:, :, 0], 0.0).then_inc(s.sem, s.step())
        dve.memset(m.reset[:, SEQ:T].rearrange("p (q w) -> p q w", w=DSEQ)[:, :, 0], 0.0).then_inc(s.sem, s.step())
        o, ka = VEC["k_a"][0], VEC["k_a"][1]
        dve.tensor_scalar(K.one_less_ka[:, :], K.vec[:, o:o + ka], -1.0, 1.0, ALU.mult, ALU.add)\
            .then_inc(s.sem, s.step("dve.low.zero"))
        dve.wait_ge(plan.dve_done, plan.value("dve.low.zero"))
        for n in range(3):
            raw, x = m.raw[n], (m.low, m.rkv[1], m.rkv[2])[n]
            dve.wait_ge(plan.act_done, plan.value(f"act.low.in{n}.{NT - 1}"))
            mid = raw[:, 1 + SEQ:].rearrange("p (q w) -> p q w", w=DSEQ + 1)
            xs = x[:, SEQ:T].rearrange("p (q w) -> p q w", w=DSEQ)
            at = 9 * (18 + n)
            dve.tensor_copy(K.last_rows[:, at:at + 1], raw[:, SEQ:SEQ + 1]).then_inc(s.sem, s.step())
            dve.tensor_copy(K.last_rows[:, at + 1:at + 9], mid[:, :, DSEQ]).then_inc(s.sem, s.step())
            dve.tensor_tensor(x[:, 0:SEQ], raw[:, 0:SEQ], raw[:, 1:1 + SEQ], ALU.subtract).then_inc(s.sem, s.step())
            dve.tensor_tensor(xs, mid[:, :, 0:DSEQ], mid[:, :, 1:], ALU.subtract)\
                .then_inc(s.sem, s.step(f"dve.low.d{n}"))
            dve.wait_ge(plan.dve_done, plan.value(f"dve.low.d{n}"))
            mu = K.column("mu", 18 + n)
            dve.scalar_tensor_tensor(out=x[:, 0:SEQ], in0=x[:, 0:SEQ], scalar=mu, in1=raw[:, 1:1 + SEQ],
                                     op0=ALU.mult, op1=ALU.add).then_inc(s.sem, s.step())
            dve.scalar_tensor_tensor(out=xs, in0=xs, scalar=mu, in1=mid[:, :, 1:], op0=ALU.mult, op1=ALU.add)\
                .then_inc(s.sem, s.step(f"dve.low.x{n}"))
        dve.wait_ge(plan.act_done, plan.value("act.low.end"))

    def pool(self, pool, before):
        K = self.K
        for n in range(3):
            slot = (n + 1) % 2
            pool.wait_ge(K.plan.sem(before[slot] if n < 2 else "pe.low.in0.2"), K.plan.value(before[slot] if n < 2 else "pe.low.in0.2"))
            K.split_weight(pool, self.w0 + n, slot)

class Banks:

    def __init__(self, plan, uses, first, count):
        self.plan, self.uses, self.first, self.count = plan, uses, first, count
        self.place = {u.split(".")[-1]: j for j, u in enumerate(uses)}

    def of(self, name):
        return self.first + self.place[name] % self.count

    def emptied(self, name, i):
        j = self.place[name]
        if j >= self.count:
            label, lag = self.uses[j - self.count], 0
        else:
            label, lag = [u for m, u in enumerate(self.uses) if m % self.count == j % self.count][-1], 1
        return self.plan.sem(label), self.plan.value(label, i, lag)


def flat(ap):
    return ap.rearrange("p a b -> p (a b)")


class MixC:

    HEADS = KC

    def __init__(self, K, w0, norm):
        self.K, self.w0, self.norm = K, w0, norm
        a = ARENA
        def take(name, shape, dtype=F32):
            nonlocal a
            t = K.at(f"c_{name}", shape, dtype, a)
            size = 4
            for n in shape[1:]:
                size *= n
            a += size
            return t
        self.q = take("q", [P, T])
        self.sig = take("sig", [P, T])
        self.i = take("i", [P, T])
        self.gate = take("gate", [P, T])
        self.qp = take("qp", [P, T])
        self.ks = take("ks", [P, T])
        self.tot = [take("tot0", [P, T]), take("tot1", [P, T // 2])]
        self.v = take("v", [P, NB + 1, P])
        self.k = take("k", [P, NB + 1, P])
        self.att = take("att", [P, NB, P])
        self.att_s = take("att_s", [NS, NS])
        self.S = take("S", [P, NB + 1, P])
        self.S_s = take("S_s", [P, NSEQ, P])
        self.v_s = take("v_s", [NS, NSEQ, P])
        self.o = take("o", [P, T])
        self.acc = take("acc", [P, T])
        assert a <= X_AT, a - X_AT
        dve = lambda n: f"dve.C.{n}"
        act = lambda n: f"act.C.{n}"
        uses = [act("vt0"), act("vt1"), act("vts"), dve("dg0"), dve("dg1"), dve("dgs")]
        for m in LEVELS:
            uses += [dve(f"m{m}_0"), dve(f"m{m}_1")] + ([dve(f"m{m}_s")] if m < DSEQ else [])
        uses += [act("kt0"), act("kt1"), act("kts"), dve("kv0"), dve("kv1"), dve("ss0"), dve("ss1"),
                 act("o0"), act("o1"), act("os")]
        self.banks = Banks(K.plan, uses, 3, 5)
        self.gemm = [(n, c) for n in range(4) for c in range(NT)]

    def chunk(self, pe, m, i, tile):
        K, plan = self.K, self.K.plan
        n, c = self.gemm[m]
        if c == 0:
            K.weight_ready(pe, tile + n)
        if m >= NT:
            nn, cc = self.gemm[m - NT]
            pe.wait_ge(plan.act_done, plan.value(f"act.C.in{nn}.{cc}", i))
            plan.alone(pe, i)
        elif not (isinstance(i, int) and i == 0):
            pe.wait_ge(plan.act_done, plan.value(f"act.C.in3.{c}", i, 1))
            plan.alone(pe, i)
        K.product(pe, n % 2, m % NT, c).then_inc(plan.steps["pe"].sem, plan.steps["pe"].step(f"pe.C.in{n}.{c}"))

    def pe(self, pe):
        K, plan, ps = self.K, self.K.plan, self.K.psum
        s = plan.steps["pe"]
        B = self.banks
        with s.loop(pe, self.HEADS) as i:
            tile = i * 4 + self.w0
            for c in range(NT):
                self.norm.wait_chunk(pe, c)
            for m in range(len(self.gemm)):
                self.chunk(pe, m, i, tile)

            def turn(src, name, after):
                for g in range(2):
                    pe.wait_ge(*B.emptied(f"{name}{g}", i))
                    plan.alone(pe, i)
                    for l in after:
                        pe.wait_ge(plan.sem(l), plan.value(l, i))
                        plan.alone(pe, i)
                    for j in range(4):
                        b = 4 * g + j
                        last = pe.transpose(ps[:, B.of(f"{name}{g}"), j * P:(j + 1) * P],
                                            src[:, b * P:(b + 1) * P], K.ident[:, :])
                    last.then_inc(s.sem, s.step(f"pe.C.{name}{g}"))
                pe.wait_ge(*B.emptied(f"{name}s", i))
                plan.alone(pe, i)
                pe.transpose(ps[0:NS, B.of(f"{name}s"), 0:P], src[:, SEQ:T], K.ident[:, :])\
                    .then_inc(s.sem, s.step(f"pe.C.{name}s"))

            turn(self.i, "vt", [f"act.C.in2.{NT - 1}"])

            def pairs(name, k, q, sample, after):
                for g in range(2):
                    pe.wait_ge(*B.emptied(f"{name}{g}", i))
                    plan.alone(pe, i)
                    for l in after:
                        pe.wait_ge(plan.sem(l), plan.value(l, i))
                        plan.alone(pe, i)
                    for j in range(4):
                        t = slice((4 * g + j) * P, (4 * g + j + 1) * P)
                        last = pe.matmul(ps[:, B.of(f"{name}{g}"), j * P:(j + 1) * P], k[:, t], q[:, t],
                                         start=True, stop=True)
                    last.then_inc(s.sem, s.step(f"pe.C.{name}{g}"))
                if sample:
                    pe.wait_ge(*B.emptied(f"{name}s", i))
                    plan.alone(pe, i)
                    pe.matmul(ps[0:NS, B.of(f"{name}s"), 0:NS], k[:, SEQ:T], q[:, SEQ:T],
                              start=True, stop=True).then_inc(s.sem, s.step(f"pe.C.{name}s"))

            pairs("dg", self.ks, self.q, True, ["dve.C.k"])
            for n, m in enumerate(LEVELS):
                pairs(f"m{m}_", self.ks, self.qp, m < DSEQ,
                      ["dve.C.qp"] if n == 0 else [f"dve.C.ks{LEVELS[n - 1]}"])
            turn(self.ks, "kt", ["dve.C.ks64"])
            for g in range(2):
                pe.wait_ge(*B.emptied(f"kv{g}", i))
                plan.alone(pe, i)
                pe.wait_ge(plan.act_done, plan.value(f"act.C.kt{g}", i))
                plan.alone(pe, i)
                pe.wait_ge(plan.act_done, plan.value(f"act.C.vt{g}", i))
                plan.alone(pe, i)
                for j in range(4):
                    b = 4 * g + j
                    last = pe.matmul(ps[:, B.of(f"kv{g}"), j * P:(j + 1) * P], self.k[:, b], self.v[:, b],
                                     start=True, stop=True)
                last.then_inc(s.sem, s.step(f"pe.C.kv{g}"))
            pe.wait_ge(plan.act_done, plan.value("act.C.kts", i))
            plan.alone(pe, i)
            pe.wait_ge(plan.dve_done, plan.value("dve.C.v_s", i))
            plan.alone(pe, i)
            for g in range(2):
                pe.wait_ge(*B.emptied(f"ss{g}", i))
                plan.alone(pe, i)
                pe.matmul(ps[:, B.of(f"ss{g}"), :], self.k[0:NS, NB],
                          flat(self.v_s[:, 4 * g:4 * g + 4]), start=True, stop=True)\
                    .then_inc(s.sem, s.step(f"pe.C.ss{g}"))
            for g in range(2):
                pe.wait_ge(*B.emptied(f"o{g}", i))
                plan.alone(pe, i)
                pe.wait_ge(plan.dve_done, plan.value(f"dve.C.S{4 * g + 3}", i))
                plan.alone(pe, i)
                if g == 0:
                    pe.wait_ge(plan.dve_done, plan.value("dve.C.m64_1", i))
                    plan.alone(pe, i)
                for j in range(4):
                    b = 4 * g + j
                    out = ps[:, B.of(f"o{g}"), j * P:(j + 1) * P]
                    pe.matmul(out, self.v[:, b], self.att[:, b], start=True, stop=False)
                    last = pe.matmul(out, self.S[:, b], self.qp[:, b * P:(b + 1) * P], start=False, stop=True)
                last.then_inc(s.sem, s.step(f"pe.C.o{g}"))
            pe.wait_ge(*B.emptied("os", i))
            plan.alone(pe, i)
            pe.wait_ge(K.sem("c_state_loaded"), (i + 1) * 16)
            out = ps[:, B.of("os"), 0:NS]
            pe.matmul(out, self.v[0:NS, NB], self.att_s[:, :], start=True, stop=True)
            for q in range(NSEQ):
                last = pe.matmul(ps[:, B.of("os"), DSEQ * q:DSEQ * q + DSEQ], self.S_s[:, q],
                                 self.qp[:, SEQ + DSEQ * q:SEQ + DSEQ * q + DSEQ], start=False,
                                 stop=True, skip_group_check=True)
            last.then_inc(s.sem, s.step("pe.C.os"))

    def act(self, act):
        K, plan, ps = self.K, self.K.plan, self.K.psum
        s = plan.steps["act"]
        B = self.banks
        for name in ("c_prompt_state_stored", "c_state_stored", "c_o_stored", "c_gate_stored"):
            act.sem_inc(K.sem(name), 16)
        with s.loop(act, self.HEADS) as i:
            act.wait_ge(K.sem("c_state_stored"), (i + 1) * 16)
            act.dma_start(flat(self.S_s[:, :]),
                          K.io["state_c"][bass.ds(i, 1)].rearrange("o p n -> (o p) n")).then_inc(K.sem("c_state_loaded"), 16)
            for m, (n, c) in enumerate(self.gemm):
                dst = (self.q, self.sig, self.i, self.gate)[n]
                func = (ACT.Silu, ACT.Sigmoid, ACT.Copy, ACT.Silu)[n]
                act.wait_ge(plan.pe_done, plan.value(f"pe.C.in{n}.{c}", i))
                plan.alone(act, i)
                if c == 0:
                    if n == 3:
                        act.wait_ge(K.sem("c_gate_stored"), (i + 1) * 16)
                    else:
                        for l in (["pe.C.dgs", "dve.C.qp"], ["dve.C.f"], ["pe.C.vts"])[n]:
                            act.wait_ge(plan.sem(l), plan.value(l, i, 1))
                            plan.alone(act, i)
                act.activation(dst[:, c * TC:(c + 1) * TC], ps[:, m % NT, 0:TC], func)\
                    .then_inc(s.sem, s.step(f"act.C.in{n}.{c}"))
            act.wait_ge(plan.act_done, plan.value(f"act.C.in3.{NT - 1}", i))
            plan.alone(act, i)
            act.dma_start(K.io["c_gate"][bass.ds(i, 1)].rearrange("o p t -> (o p) t"), self.gate[:, :])\
                .then_inc(K.sem("c_gate_stored"), 16)

            def turned(dst, name, read):
                for g in range(2):
                    act.wait_ge(plan.pe_done, plan.value(f"pe.C.{name}{g}", i))
                    plan.alone(act, i)
                    if g == 0:
                        for l in read:
                            act.wait_ge(plan.sem(l), plan.value(l, i, 1))
                            plan.alone(act, i)
                    act.activation(flat(dst[:, 4 * g:4 * g + 4]), ps[:, B.of(f"{name}{g}"), :], ACT.Copy)\
                        .then_inc(s.sem, s.step(f"act.C.{name}{g}"))
                act.wait_ge(plan.pe_done, plan.value(f"pe.C.{name}s", i))
                plan.alone(act, i)
                act.activation(dst[0:NS, NB], ps[0:NS, B.of(f"{name}s"), 0:P], ACT.Copy)\
                    .then_inc(s.sem, s.step(f"act.C.{name}s"))

            turned(self.v, "vt", ["pe.C.os", "dve.C.v_s"])
            turned(self.k, "kt", ["pe.C.ss1"])
            act.wait_ge(K.sem("c_o_stored"), (i + 1) * 16)
            act.wait_ge(plan.dve_done, plan.value("dve.C.acc", i, 1))
            plan.alone(act, i)
            for g in range(2):
                act.wait_ge(plan.pe_done, plan.value(f"pe.C.o{g}", i))
                plan.alone(act, i)
                act.activation(self.o[:, 4 * g * P:4 * (g + 1) * P], ps[:, B.of(f"o{g}"), :], ACT.Copy)\
                    .then_inc(s.sem, s.step(f"act.C.o{g}"))
            act.wait_ge(plan.pe_done, plan.value("pe.C.os", i))
            plan.alone(act, i)
            act.activation(self.o[:, SEQ:T], ps[:, B.of("os"), 0:NS], ACT.Copy).then_inc(s.sem, s.step("act.C.os"))
            act.wait_ge(plan.act_done, plan.value("act.C.os", i))
            plan.alone(act, i)
            act.dma_start(K.io["c_o"][bass.ds(i, 1)].rearrange("o p t -> (o p) t"), self.o[:, :])\
                .then_inc(K.sem("c_o_stored"), 16)
            act.wait_ge(plan.dve_done, plan.value(f"dve.C.S{NB}", i))
            plan.alone(act, i)
            act.dma_start(K.io["p_c"][bass.ds(i, 1)].rearrange("o p n -> (o p) n"), self.S[:, NB])\
                .then_inc(K.sem("c_prompt_state_stored"), 16)
            act.wait_ge(plan.dve_done, plan.value(f"dve.C.ns{NSEQ - 1}", i))
            plan.alone(act, i)
            act.dma_start(K.io["s_c"][bass.ds(i, 1)].rearrange("o p n -> (o p) n"), flat(self.S_s[:, :]))\
                .then_inc(K.sem("c_state_stored"), 16)
        for name in ("c_prompt_state_stored", "c_state_stored", "c_o_stored", "c_gate_stored"):
            act.wait_ge(K.sem(name), (self.HEADS + 1) * 16)

    def dve(self, dve):
        K, plan, ps = self.K, self.K.plan, self.K.psum
        s = plan.steps["dve"]
        B = self.banks
        for t, l in ((self.att[:], None), (self.att_s[:], None), (self.S[:, 0], None), (self.acc[:], "dve.C.zero")):
            dve.memset(t, 0.0).then_inc(s.sem, s.step(l))
        dve.wait_ge(plan.dve_done, plan.value("dve.C.zero"))
        lb = K.derived
        with s.loop(dve, self.HEADS) as i:
            f = self.tot[0]
            dve.wait_ge(plan.act_done, plan.value(f"act.C.in1.{NT - 1}", i))
            plan.alone(dve, i)
            dve.wait_ge(plan.dve_done, plan.before("dve.C.f", i))
            plan.alone(dve, i)
            dve.tensor_scalar(f[:, :], self.sig[:, :], K.derived[:, bass.ds(i + 16, 1)],
                              K.derived[:, bass.ds(i + 8, 1)], ALU.mult, ALU.add).then_inc(s.sem, s.step("dve.C.f"))
            dve.wait_ge(plan.dve_done, plan.value("dve.C.f", i))
            plan.alone(dve, i)
            dve.wait_ge(plan.pe_done, plan.value("pe.C.kts", i, 1))
            plan.alone(dve, i)
            dve.tensor_scalar(self.ks[:, :], f[:, :], -1.0, 1.0, ALU.mult, ALU.add).then_inc(s.sem, s.step("dve.C.k"))
            dve.wait_ge(plan.pe_done, plan.value("pe.C.os", i, 1))
            plan.alone(dve, i)
            dve.tensor_tensor(self.qp[:, :], self.q[:, :], f[:, :], ALU.mult).then_inc(s.sem, s.step("dve.C.qp"))

            def pick(name, mask, sample):
                if name == "dg":
                    dve.wait_ge(plan.pe_done, plan.value("pe.C.os", i, 1))
                    plan.alone(dve, i)
                    dve.wait_ge(plan.pe_done, plan.value("pe.C.dgs", i))
                    plan.alone(dve, i)
                for g in range(2):
                    dve.copy_predicated(self.att[:, 4 * g:4 * g + 4],
                                        K.masks[:, mask].unsqueeze(1).broadcast_to([P, 4, P]),
                                        ps[:, B.of(f"{name}{g}"), :].rearrange("p (j t) -> p j t", j=4))\
                        .then_inc(s.sem, s.step(f"dve.C.{name}{g}"))
                if sample:
                    dve.copy_predicated(self.att_s[:, :], K.masks[0:NS, mask, 0:NS],
                                        ps[0:NS, B.of(f"{name}s"), 0:NS]).then_inc(s.sem, s.step(f"dve.C.{name}s"))

            pick("dg", DIAG, True)
            for n, m in enumerate(LEVELS):
                width = T if m < DSEQ else SEQ
                pairs = width // (2 * m)
                tot, nxt = self.tot[n % 2], self.tot[(n + 1) % 2]
                halves = lambda t, w: t[:, 0:width].rearrange("p (b h x) -> p b h x", h=2, x=m)[:, :, w]
                sums = tot[:, 0:2 * pairs].rearrange("p (b h) -> p b h", h=2)
                dve.wait_ge(plan.pe_done, plan.value(f"pe.C.m{m}_{'s' if m < DSEQ else 1}", i))
                plan.alone(dve, i)
                dve.wait_ge(plan.dve_done, plan.before(f"dve.C.qp{m}", i))
                plan.alone(dve, i)
                second = lambda w: sums[:, :, w:w + 1].broadcast_to([P, pairs, m])
                dve.tensor_tensor(halves(self.qp, 1), halves(self.qp, 1), second(0), ALU.mult)\
                    .then_inc(s.sem, s.step(f"dve.C.qp{m}"))
                dve.tensor_tensor(halves(self.ks, 0), halves(self.ks, 0), second(1), ALU.mult)\
                    .then_inc(s.sem, s.step(f"dve.C.ks{m}"))
                dve.tensor_tensor(nxt[:, 0:pairs], sums[:, :, 0], sums[:, :, 1], ALU.mult)\
                    .then_inc(s.sem, s.step(f"dve.C.tot{m}"))
                if m == DSEQ // 2:
                    dve.wait_ge(plan.dve_done, plan.value(f"dve.C.tot{m}", i))
                    plan.alone(dve, i)
                    dve.tensor_copy(K.derived[:, 24:32], nxt[:, SEQ // DSEQ:T // DSEQ])\
                        .then_inc(s.sem, s.step("dve.C.tot_s"))
                pick(f"m{m}_", LEVELS.index(m), m < DSEQ)
            tot = self.tot[len(LEVELS) % 2]
            dve.wait_ge(plan.act_done, plan.value("act.C.vts", i))
            plan.alone(dve, i)
            dve.wait_ge(plan.pe_done, plan.value("pe.C.ss1", i, 1))
            plan.alone(dve, i)
            dve.tensor_tensor(self.v_s[:, :, :], self.v[0:NS, NB].unsqueeze(1).broadcast_to([NS, NSEQ, P]),
                              K.seq_mask[:, :].unsqueeze(2).broadcast_to([NS, NSEQ, P]), ALU.mult)\
                .then_inc(s.sem, s.step("dve.C.v_s"))
            dve.wait_ge(plan.pe_done, plan.value("pe.C.os", i, 1))
            plan.alone(dve, i)
            act_wait = K.sem("c_prompt_state_stored")
            dve.wait_ge(act_wait, (i + 1) * 16)
            for b in range(NB):
                if b % 4 == 0:
                    dve.wait_ge(plan.pe_done, plan.value(f"pe.C.kv{b // 4}", i))
                    plan.alone(dve, i)
                dve.wait_ge(plan.dve_done, plan.before(f"dve.C.S{b + 1}", i))
                plan.alone(dve, i)
                label = f"dve.C.S{b + 1}"
                dve.scalar_tensor_tensor(out=self.S[:, b + 1], in0=self.S[:, b], scalar=tot[:, b:b + 1],
                                         in1=ps[:, B.of(f"kv{b // 4}"), (b % 4) * P:(b % 4 + 1) * P],
                                         op0=ALU.mult, op1=ALU.add).then_inc(s.sem, s.step(label))
                if b % 4 == 3:
                    K.known_alias(f"dve.C.kv{b // 4}", label)
            dve.wait_ge(plan.pe_done, plan.value("pe.C.os", i))
            plan.alone(dve, i)
            for q in range(NSEQ):
                if q % 4 == 0:
                    dve.wait_ge(plan.pe_done, plan.value(f"pe.C.ss{q // 4}", i))
                    plan.alone(dve, i)
                dve.scalar_tensor_tensor(out=self.S_s[:, q], in0=self.S_s[:, q],
                                         scalar=K.derived[:, 24 + q:25 + q],
                                         in1=ps[:, B.of(f"ss{q // 4}"), (q % 4) * P:(q % 4 + 1) * P],
                                         op0=ALU.mult, op1=ALU.add).then_inc(s.sem, s.step(f"dve.C.ns{q}"))
                if q % 4 == 3:
                    K.known_alias(f"dve.C.ss{q // 4}", f"dve.C.ns{q}")
            dve.wait_ge(plan.act_done, plan.value("act.C.os", i))
            plan.alone(dve, i)
            dve.wait_ge(plan.dve_done, plan.before("dve.C.sq", i))
            plan.alone(dve, i)
            dve.tensor_tensor(self.tot[0][:, :], self.o[:, :], self.o[:, :], ALU.mult)\
                .then_inc(s.sem, s.step("dve.C.sq"))
            dve.wait_ge(plan.dve_done, plan.value("dve.C.sq", i))
            plan.alone(dve, i)
            dve.tensor_tensor(self.acc[:, :], self.acc[:, :], self.tot[0][:, :], ALU.add)\
                .then_inc(s.sem, s.step("dve.C.acc"))

    def pool(self, pool, before):
        K = self.K
        with K.plan.steps["pool"].loop(pool, self.HEADS) as i:
            for n in range(4):
                if n >= 2:
                    pool.wait_ge(K.plan.pe_done, K.plan.value(f"pe.C.in{n - 2}.{NT - 1}", i))
                    K.plan.alone(pool, i)
                else:
                    pool.wait_ge(K.plan.pe_done, K.plan.value(f"pe.C.in{n + 2}.{NT - 1}", i, 1))
                    K.plan.alone(pool, i)
                    pool.wait_ge(K.plan.sem(before[n]), K.plan.value(before[n]))
                K.split_weight(pool, i * 4 + (self.w0 + n), n % 2)


class Project:
    def __init__(self, K, name, w0, source, ready, gate=None, acc=None, gain=None, scratch=ARENA):
        self.K, self.n, self.w0, self.source, self.ready = K, name, w0, source, ready
        self.gate, self.acc, self.gain = gate, acc, gain
        self.h = K.at(f"{name}_h", [P, 2, T], F32, scratch)
        self.g = K.at(f"{name}_g", [P, 2, T], F32, scratch + 2 * WIDE)
        self.rstd = K.at(f"{name}_rstd", [P, NT, TC], F32, scratch + 4 * WIDE)

    def act(self, act):
        K, n, plan = self.K, self.n, self.K.plan
        s = plan.steps["act"]
        for label in self.ready:
            act.wait_ge(plan.sem(label), plan.value(label))
        loaded = K.sem(f"{n}_h_loaded"), K.sem(f"{n}_g_loaded")

        def load(k):
            if k >= 2:
                act.wait_ge(plan.dve_done, plan.value(f"dve.{n}.lo{k - 2}"))
            act.dma_start(self.h[:, k % 2], K.io[self.source][k]).then_inc(loaded[k % 2], 16)
            if self.gate:
                act.dma_start(self.g[:, k % 2], K.io[self.gate][k]).then_inc(loaded[k % 2], 16)

        load(0)
        load(1)
        if self.gate:
            for c in range(NT):
                act.wait_ge(plan.pe_done, plan.value(f"pe.{n}.sum{c}"))
                act.activation(self.rstd[:, c], K.psum[:, c, 0:TC], ACT.Sqrt, bias=K.derived[:, 0:1],
                               scale=1.0 / D).then_inc(s.sem, s.step(f"act.{n}.rms{c}"))
        for k in range(KC):
            if self.gate:
                act.wait_ge(plan.dve_done, plan.value(f"dve.{n}.h{k}"))
            else:
                act.wait_ge(loaded[k % 2], (k // 2 + 1) * 16)
            act.activation(K.act_hi[:, k], self.h[:, k % 2], ACT.Copy).then_inc(s.sem, s.step(f"act.{n}.hi{k}"))
            if k + 2 < KC:
                load(k + 2)

    def dve(self, dve, x_ready=()):
        K, n, plan = self.K, self.n, self.K.plan
        s = plan.steps["dve"]
        loaded = K.sem(f"{n}_h_loaded"), K.sem(f"{n}_g_loaded")
        if self.gate:
            for c in range(NT):
                dve.wait_ge(plan.act_done, plan.value(f"act.{n}.rms{c}"))
                dve.reciprocal(self.rstd[:, c], self.rstd[:, c]).then_inc(s.sem, s.step(f"dve.{n}.rstd{c}"))
            dve.wait_ge(plan.dve_done, plan.value(f"dve.{n}.rstd{NT - 1}"))
        for k in range(KC):
            if self.gate:
                dve.wait_ge(loaded[k % 2], (k // 2 + 1) * 32)
                dve.scalar_tensor_tensor(out=self.h[:, k % 2], in0=self.h[:, k % 2],
                                         scalar=K.column(self.gain, k), in1=flat(self.rstd[:, :]),
                                         op0=ALU.mult, op1=ALU.mult).then_inc(s.sem, s.step(f"dve.{n}.n{k}"))
                dve.wait_ge(plan.dve_done, plan.value(f"dve.{n}.n{k}"))
                dve.tensor_tensor(self.h[:, k % 2], self.h[:, k % 2], self.g[:, k % 2], ALU.mult)\
                    .then_inc(s.sem, s.step(f"dve.{n}.h{k}"))
            dve.wait_ge(plan.act_done, plan.value(f"act.{n}.hi{k}"))
            dve.tensor_tensor(K.act_lo[:, k], self.h[:, k % 2], K.act_hi[:, k].bitcast(F32),
                              ALU.subtract).then_inc(s.sem, s.step(f"dve.{n}.lo{k}"))
        for sem, value in x_ready:
            dve.wait_ge(sem, value)
        with s.loop(dve, KC // 2) as i:
            for j in range(2):
                for c in range(NT):
                    dve.wait_ge(plan.pe_done, plan.value(f"pe.{n}.out{j}.{c}", i))
                    plan.alone(dve, i)
                    x = K.x[:, bass.ds(i * 2 + j, 1), c * TC:(c + 1) * TC].rearrange("p o t -> p (o t)")
                    dve.tensor_tensor(x, x, K.psum[:, c + NT * j, 0:TC], ALU.add)\
                        .then_inc(s.sem, s.step(f"dve.{n}.add{j}.{c}"))

    def pe(self, pe):
        K, n, plan = self.K, self.n, self.K.plan
        if self.gate:
            for label in self.ready:
                pe.wait_ge(plan.sem(label), plan.value(label))
            for c in range(NT):
                pe.matmul(K.psum[:, c, 0:TC], K.ones[:, :], self.acc[:, c * TC:(c + 1) * TC],
                          start=True, stop=True)\
                    .then_inc(plan.steps["pe"].sem, plan.steps["pe"].step(f"pe.{n}.sum{c}"))
            pe.wait_ge(plan.dve_done, plan.value(f"dve.{n}.rstd{NT - 1}"))
        pe.wait_ge(plan.dve_done, plan.value(f"dve.{n}.lo{KC - 1}"))
        with plan.steps["pe"].loop(pe, KC // 2) as i:
            for j in range(2):
                K.weight_ready(pe, i * 2 + (self.w0 + j))
                for c in range(NT):
                    pe.wait_ge(plan.dve_done, plan.value(f"dve.{n}.add{j}.{c}", i, 1))
                    plan.alone(pe, i)
                    K.product(pe, j, c + NT * j, c)\
                        .then_inc(plan.steps["pe"].sem, plan.steps["pe"].step(f"pe.{n}.out{j}.{c}"))

    def pool(self, pool, before):
        K, n = self.K, self.n
        with K.plan.steps["pool"].loop(pool, KC // 2) as i:
            for j in range(2):
                pool.wait_ge(K.plan.pe_done, K.plan.value(f"pe.{n}.out{j}.{NT - 1}", i, 1))
                K.plan.alone(pool, i)
                pool.wait_ge(K.plan.sem(before[j]), K.plan.value(before[j]))
                K.split_weight(pool, i * 2 + (self.w0 + j), j)


INPUTS = (("x_in", (P, KC, T), F32), ("weights", (215, P, KC * P), F32), ("vec", (P, NVEC), F32),
          ("ident", (P, P), F32), ("half_ones", (P, P), F32), ("masks", (P, 21, P), F32), ("seq_mask", (NS, NSEQ), F32),
          ("ident2", (P, 64), F32), ("shift_in", (P, 8 * 21), F32),
          ("low_w", (6, P, 3 * P), F32), ("state_b", (6, P, NSEQ * 64), F32), ("state_c", (KC, P, NSEQ * P), F32),
          ("rel_bias", (32, 12), F32), ("onehot", (32, 3, REL), F32), ("outside", (4, 3, REL), F32),
          ("cache_a0", (NSEQ, 128, 512), F32), ("cache_a1", (NSEQ, 512, 512), F32), ("cache_a2", (NSEQ, 2048, 512), F32))
OUTPUTS = (("y", (P, KC, T)), ("kv", (3, 4, P, T)), ("last", (P, 9 * 21)), ("p_wkv", (6, P, 64)),
           ("s_wkv", (6, P, NSEQ * 64)), ("p_c", (KC, P, P)), ("s_c", (KC, P, NSEQ * P)))
SCRATCH = (("mix", (KC, P, T)), ("b_gd", (2, P, T)), ("c_gate", (KC, P, T)), ("c_o", (KC, P, T)),
           ("rows", (3, 3, NS, 2 * P)), ("rel_rows", (3, 4, REL)),
           ("bias_rows", (3, P, 4 * REL)), ("og_rows", (2, SEQ, ROW_A)))


def program(nc, io, known):
    with ExitStack() as ctx:
        K = Kernel(nc, ctx, io, known)
        setup = Setup()
        norm_mix0 = Norm(K, "nm0", "norm_mix0", ["dve.setup.masks"], ["dve.A.rel2"])
        attention = MixA(K, 0, norm_mix0)
        sample_attention = SampleA(K)
        w0 = TILES_A
        rwkv = MixB(K, w0 + TILES_LORA)
        low_rank = LowRank(K, w0, rwkv)
        w0 += TILES_LORA + TILES_B
        out0 = Project(K, "out0", w0, "mix", ["dve.B.out", "dve.B.sS", "pe.B.ys", "pe.B.var2", "act.B.var2"])
        w0 += TILES_OUT
        norm_mlp0 = Norm(K, "nf0", "norm_mlp0", [f"dve.out0.add1.{NT - 1}"], [f"pe.out0.out1.{NT - 1}"])
        mlp0 = MLP(K, "ff0", w0, norm_mlp0)
        w0 += TILES_MLP
        norm_mix1 = Norm(K, "nm1", "norm_mix1", mlp0.end(), [mlp0.pe_end()])
        hgrn = MixC(K, w0, norm_mix1)
        w0 += TILES_C
        out1 = Project(K, "out1", w0, "c_o", ["dve.C.acc", "act.C.os"], gate="c_gate", acc=hgrn.acc, gain="c_norm")
        w0 += TILES_OUT
        norm_mlp1 = Norm(K, "nf1", "norm_mlp1", [f"dve.out1.add1.{NT - 1}"], [f"pe.out1.out1.{NT - 1}"])
        mlp1 = MLP(K, "ff1", w0, norm_mlp1)
        w0 += TILES_MLP
        final = FinalNorm(K, "end", "norm_final", mlp1.end(), [])
        tiles = w0
        block = ctx.enter_context(nc.Block())

        @block.sync
        def _(sp):
            K.load_weight(sp, 0)
            with sp.Fori(1, tiles) as n:
                K.load_weight(sp, n)

        @block.gpsimd
        def _(pool):
            K.plan.steps["pool"].begin(pool)
            pool.wait_ge(K.plan.dve_done, K.plan.value("dve.setup.zero"))
            attention.pool(pool)
            low_rank.pool(pool, ["pe.A2.in5.2", "pe.A2.in4.2"])
            rwkv.pool(pool, ["pe.low.in1.2", "pe.low.in2.2", None])
            out0.pool(pool, [f"pe.B.in{j}.{NT - 1}" for j in range(2)])
            mlp0.pool(pool, [f"pe.out0.out{j}.{NT - 1}" for j in range(2)])
            hgrn.pool(pool, [mlp0.pe_end() for j in range(2)])
            out1.pool(pool, [f"pe.C.in{2 + j}.{NT - 1}" for j in range(2)])
            mlp1.pool(pool, [f"pe.out1.out{j}.{NT - 1}" for j in range(2)])

        @block.scalar
        def _(act):
            K.plan.steps["act"].begin(act)
            attention.bias_act(act)
            act.dma_start(K.x[:], io["x_in"]).then_inc(K.sem("x_loaded"), 16)
            setup.act(act, K)
            act.wait_ge(K.sem("x_loaded"), 16)
            norm_mix0.act(act)
            attention.act(act)
            sample_attention.act(act)
            low_rank.act(act)
            rwkv.act(act)
            act.dma_start(io["last"], K.last_rows[:]).then_inc(K.sem("last_stored"), 16)
            for label in out0.ready:
                act.wait_ge(K.plan.sem(label), K.plan.value(label))
            act.dma_start(K.x[:], io["x_in"]).then_inc(K.sem("x_loaded"), 16)
            out0.act(act)
            norm_mlp0.act(act)
            mlp0.act(act)
            norm_mix1.act(act)
            hgrn.act(act)
            out1.act(act)
            norm_mlp1.act(act)
            mlp1.act(act)
            final.act(act)
            act.wait_ge(K.sem("last_stored"), 16)

        @block.vector
        def _(dve):
            K.plan.steps["dve"].begin(dve)
            attention.bias_dve(dve)
            setup.dve(dve, K)
            dve.wait_ge(K.sem("x_loaded"), 16)
            norm_mix0.dve(dve)
            attention.dve(dve)
            sample_attention.dve(dve)
            dve.wait_ge(K.sem("s_mix_stored"), 16)
            low_rank.dve(dve)
            rwkv.dve(dve)
            out0.dve(dve, [(K.sem("x_loaded"), 32)])
            norm_mlp0.dve(dve)
            mlp0.dve(dve)
            norm_mix1.dve(dve)
            dve.wait_ge(K.plan.dve_done, K.plan.value(f"dve.nm1.lo{KC * NT - 1}"))
            hgrn.dve(dve)
            out1.dve(dve)
            norm_mlp1.dve(dve)
            mlp1.dve(dve)
            final.dve(dve)

        @block.tensor
        def _(pe):
            K.plan.steps["pe"].begin(pe)
            attention.bias_pe(pe)
            norm_mix0.pe(pe)
            norm_mix0.wait_chunk(pe, NT - 1)
            attention.pe(pe)
            sample_attention.pe(pe)
            low_rank.pe(pe)
            rwkv.pe(pe)
            out0.pe(pe)
            norm_mlp0.pe(pe)
            mlp0.pe(pe)
            norm_mix1.pe(pe)
            hgrn.pe(pe)
            out1.pe(pe)
            norm_mlp1.pe(pe)
            mlp1.pe(pe)
            final.pe(pe)


def build(nc, known):
    io = {name: nc.dram_tensor(name, shape, dtype, kind="ExternalInput").ap() for name, shape, dtype in INPUTS}
    for name, shape in OUTPUTS:
        io[name] = nc.dram_tensor(name, shape, F32, kind="ExternalOutput").ap()
    for name, shape in SCRATCH:
        io[name] = nc.dram_tensor(name, shape, F32, kind="Internal").ap()
    program(nc, io, known)


def feature_major(prompt, samples):
    x = np.concatenate([prompt.reshape(SEQ, -1), samples.reshape(NS, -1)], 0)
    return np.ascontiguousarray(x.T.reshape(-1, P, T).transpose(1, 0, 2))


def weight_tiles(w):
    n = w.shape[1] // P
    return w.reshape(-1, P, n, P).transpose(2, 1, 0, 3).reshape(n, P, -1)


def padded(x, width):
    return np.concatenate([x, np.zeros(x.shape[:-1] + (width - x.shape[-1],), x.dtype)], -1)


def attention_tiles(w):
    t = weight_tiles(w)
    return np.concatenate([t[[2 * g, 2 * g + 1, 6 + 2 * g, 7 + 2 * g, 12 + 2 * g, 13 + 2 * g]] for g in range(3)])


def rwkv_tiles(w):
    t = weight_tiles(padded(w, 21 * P))
    return np.concatenate([t[18:21]] + [t[[i, 6 + i, 12 + i]] for i in range(6)])


def mlp_tiles(up, down):
    up, down = weight_tiles(up), down.reshape(FF_TILES, P, D)
    order = [up[0:2]]
    for g in range(1, FF_TILES // 2):
        order += [up[2 * g:2 * g + 2], down[2 * g - 2:2 * g]]
    return np.concatenate(order + [down[FF_TILES - 2:]])


def constants():
    f = np.float32
    s, t = np.arange(P)[:, None], np.arange(P)[None]
    masks = np.zeros((P, 21, P), f)
    for n, b in enumerate(LEVELS):
        masks[:, n] = (s // (2 * b) == t // (2 * b)) & (s % (2 * b) < b) & (t % (2 * b) >= b)
        masks[:, 7 + n] = masks[:, n].T
    masks[:, DIAG], masks[:, UPPER], masks[:, UPPER_EQ], masks[:, LOWER] = s == t, s < t, s <= t, s > t
    block = s // DSEQ == t // DSEQ
    masks[:, 18], masks[:, 19], masks[:, 20] = (s < t) & block, (s <= t) & block, (s > t) & block
    onehot, outside = np.zeros((32, 3, REL), f), np.full((4, 3, REL), FAR, f)
    for g, r in enumerate(DILATION):
        j = np.arange(WINDOW + 1)
        d = j * r
        large = 16 + (np.log(np.maximum(d, 1).astype(f) / f(16)) / f(np.log(2048 / 16)) * 16).astype(np.int32)
        onehot[np.where(d < 16, d, np.minimum(large, 31)), g, 2 * P - 1 - j] = 1
        outside[:, g, 2 * P - 1 - j] = 0
    return {"ident": np.eye(P, dtype=f), "half_ones": (s // 64 == t // 64).astype(f), "masks": masks,
            "seq_mask": (np.arange(NS)[:, None] // DSEQ == np.arange(NSEQ)[None]).astype(f),
            "ident2": np.concatenate([np.eye(64, dtype=f)] * 2),
            "onehot": onehot, "outside": outside}


def lay_out(a):
    vec = np.zeros((P, NVEC), np.float32)
    named = {"norm_final": a["norm_final"], "c_norm": a["c_norm"][0]}
    for layer in range(2):
        named[f"norm_mix{layer}"], named[f"norm_mlp{layer}"] = a["norm_mix"][layer], a["norm_mlp"][layer]
        named[f"lb{layer}"] = a["c_lb_raw"][layer]
    for name in ("mu", "w0", "a0", "k_k", "k_a", "r_k", "lnx_w", "lnx_b"):
        named[name] = a["e_" + name][0]
    for name, v in named.items():
        at, n = VEC[name]
        vec[:, at:at + n] = padded(v.reshape(-1), n * P).reshape(n, P).T
    low = np.zeros((6, P, 3, P), np.float32)
    w2, a2, g2 = (a[k][0].reshape(-1, 6, P).transpose(1, 0, 2) for k in ("e_w2", "e_a2", "e_g2"))
    low[:, 0:64, 0], low[:, 64:, 0], low[:, :, 1], low[:, :32, 2] = w2, a2, g2[:, :P], g2[:, P:]
    shift = padded(a["state_b_shift"][0], 21 * P).reshape(NSEQ, 21, P).transpose(2, 1, 0).reshape(P, -1)
    weights = np.concatenate([
        attention_tiles(a["e_w_in"][0][:, :2304]), rwkv_tiles(a["e_w_in"][0][:, 2304:]), weight_tiles(a["e_w_out"][0]),
        mlp_tiles(a["mlp_up"][0], a["mlp_down"][0]),
        weight_tiles(a["c_w_in"][0]).reshape(4, KC, P, -1).transpose(1, 0, 2, 3).reshape(4 * KC, P, -1),
        weight_tiles(a["c_w_out"][0]), mlp_tiles(a["mlp_up"][1], a["mlp_down"][1])])
    out = {"x_in": feature_major(a["x_prompt"], a["x_sample"]), "weights": weights, "vec": vec, "low_w": low.reshape(6, P, -1),
           "shift_in": shift, "rel_bias": a["rel_bias"],
           "state_b": a["state_b_wkv"][0].reshape(8, 6, 2, 64, 64).transpose(1, 2, 4, 0, 3).reshape(6, P, NSEQ * 64),
           "state_c": a["state_c"][0].transpose(1, 2, 0, 3).reshape(KC, P, NSEQ * P), **constants()}
    for g, rows in enumerate((128, 512, 2048)):
        out[f"cache_a{g}"] = a[f"cache_a{g}"][0].reshape(NSEQ, rows, 512)
    return {name: np.ascontiguousarray(v) for name, v in out.items()}


def give_back(o):
    y = o["y"].transpose(2, 1, 0).reshape(T, D)
    prompt_kv, sample_kv = [], []
    for g, (r, rows) in enumerate(zip(DILATION, (128, 512, 1024))):
        kv = o["kv"][g].reshape(2, HEADS_A, HD, T)
        prompt = kv[..., :SEQ].reshape(2, HEADS_A, HD, r, SEQ // r).transpose(4, 3, 0, 1, 2).reshape(SEQ, 2, HEADS_A, HD)
        prompt_kv.append(prompt[SEQ - rows:][None, None])
        sample_kv.append(kv[..., SEQ:].transpose(3, 0, 1, 2).reshape(1, NSEQ, DSEQ, 2, HEADS_A, HD))
    last = o["last"].reshape(P, 21, 1 + NSEQ).transpose(2, 1, 0).reshape(1 + NSEQ, -1)[:, :2592]
    p_wkv = o["p_wkv"].reshape(12, 64, 64).transpose(0, 2, 1)[None, None]
    s_wkv = o["s_wkv"].reshape(6, 2, 64, NSEQ, 64).transpose(3, 0, 1, 4, 2).reshape(1, NSEQ, 12, 64, 64)
    s_c = o["s_c"].reshape(KC, P, NSEQ, P).transpose(2, 0, 1, 3)[None]
    got = (y[:SEQ][None], y[SEQ:].reshape(NSEQ, DSEQ, D), *prompt_kv, last[0:1][None], p_wkv, o["p_c"][None, None],
           *sample_kv, last[1:][None], s_wkv, s_c)
    return tuple(np.ascontiguousarray(v) for v in got)


def kernel(**inputs):
    import concourse.bacc as bacc
    from concourse.bass_utils import run_bass_kernel_spmd

    known = {}
    build(bacc.Bacc("TRN2", target_bir_lowering=False, num_devices=1), known)
    nc = bacc.Bacc("TRN2", target_bir_lowering=False, num_devices=1)
    build(nc, known)
    arrays = lay_out({name: np.asarray(v) for name, v in inputs.items()})
    result = run_bass_kernel_spmd(nc, [arrays], core_ids=[0])
    return give_back(result.results[0])
```
